# Optimizing a Trainium2 kernel written in Bass

```python
import jax
import jax.numpy as jnp
from jax import lax
import numpy as np
import math
import jax, jax.numpy as jnp

D_MODEL = 1024
BATCH = 1
SEQ = 1024
DEPTH = 1

CHUNK = 64
D_PLE = 256
N_MIXERS = 4
D_GROUP = D_MODEL // N_MIXERS
D_MIX = N_MIXERS * D_GROUP
HEAD_DIM = 64
N_GROUP_HEADS = D_GROUP // HEAD_DIM
GMLP_BLOCK = 128
DN_CONV = 4
RW_DECAY_LORA = 64
RW_AAA_LORA = 64
RW_GATE_LORA = 128
RW_LNX_EPS = 64e-5
CONF_CONV = 31
D_FF = 256 * round(8 * D_MODEL / (3 * 256))
FFN_CONV = 3
NORM_EPS = 1e-6
LN_EPS = 1e-5

A_COLS = 2 * D_GROUP
B_COLS = 4 * D_GROUP + 2 * N_GROUP_HEADS
C_COLS = 3 * D_GROUP + RW_DECAY_LORA + RW_AAA_LORA + RW_GATE_LORA
D_COLS = 2 * D_GROUP
D_IN = A_COLS + B_COLS + C_COLS + D_COLS


def _split(x, sizes):
    idx = [int(i) for i in np.cumsum(sizes)[:-1]]
    return jnp.split(x, idx, axis=-1)

def rms_norm(x, g):
    xf = x.astype(jnp.float32)
    y = xf * lax.rsqrt(jnp.mean(xf * xf, axis=-1, keepdims=True) + NORM_EPS)
    return (y * g.astype(jnp.float32)).astype(x.dtype)

def layer_norm(x, g, b, eps):
    xf = x.astype(jnp.float32)
    mu = jnp.mean(xf, axis=-1, keepdims=True)
    var = jnp.mean(jnp.square(xf - mu), axis=-1, keepdims=True)
    y = (xf - mu) * lax.rsqrt(var + eps) * g.astype(jnp.float32) + b.astype(jnp.float32)
    return y.astype(x.dtype)

def l2_normalize(x):
    xf = x.astype(jnp.float32)
    return xf * lax.rsqrt(jnp.sum(xf * xf, axis=-1, keepdims=True) + 1e-6)

def causal_depthwise_conv(x, w):
    K, C = w.shape
    return lax.conv_general_dilated(
        x, w[:, None, :].astype(x.dtype), window_strides=(1,), padding=[(K - 1, 0)],
        dimension_numbers=('NWC', 'WIO', 'NWC'), feature_group_count=C)

def _heads(t):
    Bn, S, _ = t.shape
    return t.reshape(Bn, S, N_GROUP_HEADS, HEAD_DIM)

def gmlp_spatial_gating(z, v_g, v_b, w_s, b_s):
    Bn, S, _ = z.shape
    u, v = jnp.split(jax.nn.gelu(z), 2, axis=-1)
    v = layer_norm(v, v_g, v_b, LN_EPS)
    v = v.reshape(Bn, S // GMLP_BLOCK, GMLP_BLOCK, N_GROUP_HEADS, HEAD_DIM)
    pos = jnp.arange(GMLP_BLOCK) // CHUNK
    mask = (pos[None, :] <= pos[:, None]).astype(w_s.dtype)
    sv = jnp.einsum('hij,bnjhd->bnihd', w_s * mask, v) + b_s.T[None, None, :, :, None]
    return u * sv.reshape(Bn, S, D_GROUP)

def chunk_gated_delta_rule(q, k, v, g, beta):
    Bn, S, H, Dk = q.shape
    Dv = v.shape[-1]
    N = S // CHUNK

    def chunks(t):
        t = t.reshape((Bn, N, CHUNK, H) + t.shape[3:])
        return jnp.moveaxis(t, 3, 1)

    q, k, v, beta = chunks(q), chunks(k), chunks(v), chunks(beta)
    g = jnp.cumsum(chunks(g), axis=-1)
    incl = jnp.tril(jnp.ones((CHUNK, CHUNK), dtype=bool))
    strict = jnp.tril(jnp.ones((CHUNK, CHUNK), dtype=bool), -1)
    diff = g[..., :, None] - g[..., None, :]
    decay = jnp.where(incl, jnp.exp(jnp.where(incl, diff, 0.0)), 0.0)
    kb = k * beta[..., None]
    L = jnp.where(strict, jnp.einsum('bhnid,bhnjd->bhnij', kb, k) * decay, 0.0)
    eye = jnp.eye(CHUNK, dtype=jnp.float32)
    rhs = jnp.concatenate([v * beta[..., None], kb * jnp.exp(g)[..., None]], axis=-1)
    sol = lax.linalg.triangular_solve(eye + L, rhs, left_side=True, lower=True)
    u, w = sol[..., :Dv], sol[..., Dv:]
    attn = jnp.einsum('bhnid,bhnjd->bhnij', q, k) * decay
    g_last = g[..., -1]
    k_dec = k * jnp.exp(g_last[..., None] - g)[..., None]
    q_dec = q * jnp.exp(g)[..., None]

    def step(state, inp):
        q_c, k_c, u_c, w_c, a_c, gl = inp
        v_new = u_c - jnp.einsum('bhck,bhkv->bhcv', w_c, state)
        o = jnp.einsum('bhck,bhkv->bhcv', q_c, state) + jnp.einsum('bhij,bhjv->bhiv', a_c, v_new)
        state = state * jnp.exp(gl)[..., None, None] + jnp.einsum('bhck,bhcv->bhkv', k_c, v_new)
        return state, o

    xs = tuple(jnp.moveaxis(t, 2, 0) for t in (q_dec, k_dec, u, w, attn, g_last))
    state0 = jnp.zeros((Bn, H, Dk, Dv), jnp.float32)
    _, o = lax.scan(step, state0, xs)
    o = jnp.moveaxis(jnp.moveaxis(o, 0, 2), 1, 3)
    return o.reshape(Bn, S, H, Dv)

def gated_deltanet(z, conv_w, a_log, dt_bias, o_g):
    q, k, v, gate, beta_raw, alpha_raw = _split(z, [D_GROUP] * 4 + [N_GROUP_HEADS] * 2)
    qkv = jax.nn.silu(causal_depthwise_conv(jnp.concatenate([q, k, v], axis=-1), conv_w))
    q, k, v = jnp.split(qkv, 3, axis=-1)
    q = l2_normalize(_heads(q)) * (HEAD_DIM ** -0.5)
    k = l2_normalize(_heads(k))
    v = _heads(v).astype(jnp.float32)
    beta = jax.nn.sigmoid(beta_raw.astype(jnp.float32))
    g = -jnp.exp(a_log.astype(jnp.float32)) * jax.nn.softplus(
        alpha_raw.astype(jnp.float32) + dt_bias.astype(jnp.float32))
    o = chunk_gated_delta_rule(q, k, v, g, beta)
    o = rms_norm(o, o_g) * jax.nn.silu(_heads(gate).astype(jnp.float32))
    Bn, S = z.shape[:2]
    return o.reshape(Bn, S, D_GROUP).astype(z.dtype)

def rwkv7_recurrence(r, w, k, v, a, b):
    Bn, S, H, D = r.shape

    def step(state, inp):
        r_t, w_t, k_t, v_t, a_t, b_t = inp
        sa = jnp.einsum('bhij,bhj->bhi', state, a_t)
        state = (state * w_t[:, :, None, :] + sa[..., None] * b_t[:, :, None, :]
                 + v_t[..., None] * k_t[:, :, None, :])
        return state, jnp.einsum('bhij,bhj->bhi', state, r_t)

    xs = tuple(jnp.moveaxis(t, 1, 0) for t in (r, w, k, v, a, b))
    _, y = lax.scan(step, jnp.zeros((Bn, H, D, D), jnp.float32), xs)
    return jnp.moveaxis(y, 0, 1)

def rwkv7_time_mix(P, mu, w0, w2, a0, a2, g2, k_k, k_a, r_k, lnx_g, lnx_b):
    Bn, S, _ = P.shape
    P_prev = jnp.pad(P, ((0, 0), (1, 0), (0, 0)))[:, :-1]
    P = P + (P_prev - P) * mu
    r, k, v, xw, xa, xg = _split(P, [D_GROUP] * 3 + [RW_DECAY_LORA, RW_AAA_LORA, RW_GATE_LORA])
    w = -jax.nn.softplus(-(w0 + jnp.tanh(xw) @ w2)) - 0.5
    a = jax.nn.sigmoid(a0 + xa @ a2)
    gate = jax.nn.sigmoid(xg) @ g2
    kk = l2_normalize(_heads(k * k_k))
    k = k * (1.0 + (a - 1.0) * k_a)
    r_h = _heads(r).astype(jnp.float32)
    k_h = _heads(k).astype(jnp.float32)
    v_h = _heads(v).astype(jnp.float32)
    a_h = _heads(a).astype(jnp.float32)
    decay = jnp.exp(-jnp.exp(_heads(w).astype(jnp.float32)))
    y = rwkv7_recurrence(r_h, decay, k_h, v_h, -kk, kk * a_h)
    y = layer_norm(y, lnx_g.reshape(N_GROUP_HEADS, HEAD_DIM), lnx_b.reshape(N_GROUP_HEADS, HEAD_DIM), RW_LNX_EPS)
    y = y + jnp.sum(r_h * k_h * r_k.astype(jnp.float32), axis=-1, keepdims=True) * v_h
    return (y.reshape(Bn, S, D_GROUP).astype(P.dtype) * gate)

def conformer_conv(z, conv_w, conv_b, ln_g, ln_b):
    z1, z2 = jnp.split(z, 2, axis=-1)
    h = z1 * jax.nn.sigmoid(z2)
    h = causal_depthwise_conv(h, conv_w) + conv_b
    h = layer_norm(h, ln_g, ln_b, LN_EPS)
    return jax.nn.silu(h)

def first_inputs(seed: int = 0) -> dict:
    key = jax.random.key(seed)
    ks = iter(jax.random.split(key, 40))
    f32 = jnp.float32

    def nrm(shape, scale):
        return jax.random.normal(next(ks), shape, f32) * scale

    def gain(shape):
        return 1.0 + nrm(shape, 0.02)

    L, H = DEPTH, N_GROUP_HEADS
    dt = jnp.exp(jax.random.uniform(next(ks), (L, H), f32, float(np.log(1e-3)), float(np.log(1e-1))))
    return {
        'x': nrm((BATCH, SEQ, D_MODEL), 1.0),
        'p': nrm((DEPTH, BATCH, SEQ, D_PLE), 1.0),
        'norm_mix_g': gain((L, D_MODEL)),
        'w_in': nrm((L, D_MODEL, D_IN), D_MODEL ** -0.5),
        'gmlp_v_g': gain((L, D_GROUP)),
        'gmlp_v_b': nrm((L, D_GROUP), 0.02),
        'gmlp_w_s': nrm((L, H, GMLP_BLOCK, GMLP_BLOCK), GMLP_BLOCK ** -0.5),
        'gmlp_b_s': 1.0 + nrm((L, H, GMLP_BLOCK), 0.1),
        'dn_conv_w': nrm((L, DN_CONV, 3 * D_GROUP), DN_CONV ** -0.5),
        'dn_a_log': jnp.log(jax.random.uniform(next(ks), (L, H), f32, 1.0, 16.0)),
        'dn_dt_bias': dt + jnp.log(-jnp.expm1(-dt)),
        'dn_o_g': gain((L, HEAD_DIM)),
        'rw_mu': jax.random.uniform(next(ks), (L, C_COLS), f32, 0.0, 1.0),
        'rw_w0': jax.random.uniform(next(ks), (L, D_GROUP), f32, -6.0, -1.0),
        'rw_w2': nrm((L, RW_DECAY_LORA, D_GROUP), 0.5 * RW_DECAY_LORA ** -0.5),
        'rw_a0': nrm((L, D_GROUP), 0.1),
        'rw_a2': nrm((L, RW_AAA_LORA, D_GROUP), RW_AAA_LORA ** -0.5),
        'rw_g2': nrm((L, RW_GATE_LORA, D_GROUP), RW_GATE_LORA ** -0.5),
        'rw_k_k': 0.85 + nrm((L, D_GROUP), 0.05),
        'rw_k_a': 1.0 + nrm((L, D_GROUP), 0.05),
        'rw_r_k': nrm((L, H, HEAD_DIM), 0.1),
        'rw_lnx_g': gain((L, D_GROUP)),
        'rw_lnx_b': nrm((L, D_GROUP), 0.02),
        'cf_conv_w': nrm((L, CONF_CONV, D_GROUP), CONF_CONV ** -0.5),
        'cf_conv_b': nrm((L, D_GROUP), 0.02),
        'cf_ln_g': gain((L, D_GROUP)),
        'cf_ln_b': nrm((L, D_GROUP), 0.02),
        'w_out': nrm((L, D_MIX, D_MODEL), D_MIX ** -0.5),
        'norm_ffn_g': gain((L, D_MODEL)),
        'w_ffn_gate': nrm((L, D_MODEL, D_FF), D_MODEL ** -0.5),
        'w_ffn_up': nrm((L, D_MODEL, D_FF), D_MODEL ** -0.5),
        'ffn_conv_w': nrm((L, FFN_CONV, D_FF), FFN_CONV ** -0.5),
        'w_ffn_down': nrm((L, D_FF, D_MODEL), D_FF ** -0.5),
        'norm_ple_g': gain((L, D_MODEL)),
        'w_ple_gate': nrm((L, D_MODEL, D_MODEL), D_MODEL ** -0.5),
        'w_ple_proj': nrm((L, D_PLE, D_MODEL), D_PLE ** -0.5),
        'final_norm_g': gain((D_MODEL,)),
    }

def first_block(x, p, norm_mix_g, w_in, gmlp_v_g, gmlp_v_b, gmlp_w_s, gmlp_b_s,
              dn_conv_w, dn_a_log, dn_dt_bias, dn_o_g,
              rw_mu, rw_w0, rw_w2, rw_a0, rw_a2, rw_g2, rw_k_k, rw_k_a, rw_r_k, rw_lnx_g, rw_lnx_b,
              cf_conv_w, cf_conv_b, cf_ln_g, cf_ln_b, w_out,
              norm_ffn_g, w_ffn_gate, w_ffn_up, ffn_conv_w, w_ffn_down,
              norm_ple_g, w_ple_gate, w_ple_proj, final_norm_g):
    h = x
    for i in range(DEPTH):
        hn = rms_norm(h, norm_mix_g[i])
        z_a, z_b, z_c, z_d = _split(hn @ w_in[i], [A_COLS, B_COLS, C_COLS, D_COLS])
        o_a = gmlp_spatial_gating(z_a, gmlp_v_g[i], gmlp_v_b[i], gmlp_w_s[i], gmlp_b_s[i])
        o_b = gated_deltanet(z_b, dn_conv_w[i], dn_a_log[i], dn_dt_bias[i], dn_o_g[i])
        o_c = rwkv7_time_mix(z_c, rw_mu[i], rw_w0[i], rw_w2[i], rw_a0[i], rw_a2[i], rw_g2[i],
                             rw_k_k[i], rw_k_a[i], rw_r_k[i], rw_lnx_g[i], rw_lnx_b[i])
        o_d = conformer_conv(z_d, cf_conv_w[i], cf_conv_b[i], cf_ln_g[i], cf_ln_b[i])
        h = h + jnp.concatenate([o_a, o_b, o_c, o_d], axis=-1) @ w_out[i]
        hn = rms_norm(h, norm_ffn_g[i])
        gate = causal_depthwise_conv(hn @ w_ffn_gate[i], ffn_conv_w[i])
        h = h + (jax.nn.silu(gate) * (hn @ w_ffn_up[i])) @ w_ffn_down[i]
        hn = rms_norm(h, norm_ple_g[i])
        h = h + (p[i] @ w_ple_proj[i]) * jax.nn.sigmoid(hn @ w_ple_gate[i])
    return rms_norm(h, final_norm_g)


_first_inputs = first_inputs


def first_inputs(seed=0):
    import zlib

    import numpy as np

    out = dict(_first_inputs(seed))
    spreads = {}
    factors = {'norm_mix_g': 3.409,
     'gmlp_v_g': 120.626,
     'gmlp_v_b': 113.333,
     'dn_o_g': 104.623,
     'rw_w2': 8.0,
     'rw_a0': 6.573,
     'rw_k_k': 200.0,
     'rw_k_a': 4.337,
     'rw_lnx_g': 200.0,
     'rw_lnx_b': 200.0,
     'cf_conv_b': 25.053,
     'cf_ln_g': 200.0,
     'cf_ln_b': 200.0,
     'norm_ffn_g': 13.102,
     'norm_ple_g': 200.0,
     'final_norm_g': 19.353,
     'gmlp_b_s': 22.041,
     'w_ple_gate': 21.368,
     'p': 8.0,
     'w_ple_proj': 8.0}
    for name, (base, spread) in spreads.items():
        noise = np.random.default_rng([zlib.crc32(name.encode()), seed]).standard_normal(out[name].shape)
        drawn = base * np.exp(spread * noise) if base else spread * noise
        out[name] = jnp.asarray(drawn.astype(out[name].dtype))
    for name, factor in factors.items():
        out[name] = (out[name] * factor).astype(out[name].dtype)
    return out


_narrow_inputs = first_inputs


def first_inputs(seed=0):

    out = dict(_narrow_inputs(seed))
    wider = {'gmlp_v_g': 3.09,
     'gmlp_v_b': 3.12,
     'gmlp_b_s': 3.11,
     'dn_o_g': 3.08,
     'rw_k_k': 4.84,
     'rw_lnx_g': 5.18,
     'rw_lnx_b': 5.22,
     'cf_ln_g': 4.83,
     'cf_ln_b': 4.92,
     'norm_ple_g': 3.55,
     'final_norm_g': 3.02}
    for name, times in wider.items():
        mean = out[name].mean()
        out[name] = (mean + times * (out[name] - mean)).astype(out[name].dtype)
    return out


MEM_LEN = 256
D_MIX_2 = D_MODEL
SSD_WIDTH = D_MIX_2 // 2
SSD_HEAD_DIM = 64
SSD_HEADS = SSD_WIDTH // SSD_HEAD_DIM
SSD_GROUPS = 2
SSD_HEADS_PER_GROUP = SSD_HEADS // SSD_GROUPS
SSD_STATE = 128
SSD_CONV = 4
SSD_CHUNK = 128
SSD_XBC = SSD_WIDTH + 2 * SSD_GROUPS * SSD_STATE

S5_WIDTH = D_MIX_2 // 4
S5_GROUP_CH = 16
S5_GROUPS = S5_WIDTH // S5_GROUP_CH
S5_STATE = 64

RG_WIDTH = D_MIX_2 - SSD_WIDTH - S5_WIDTH
RG_BLOCKS = 4
RG_BLOCK_DIM = RG_WIDTH // RG_BLOCKS
RG_CONV = 4
RG_C = 8.0

XA_HEADS = 4
XA_HEAD_DIM = D_MODEL // XA_HEADS
D_FF_2 = 4 * D_MODEL

ALPHA = (2.0 * DEPTH) ** 0.25
BETA = (8.0 * DEPTH) ** -0.25

IN_COLS = (SSD_WIDTH, SSD_XBC, SSD_HEADS, S5_WIDTH, RG_WIDTH, RG_WIDTH)
D_IN_2 = SSD_WIDTH + SSD_XBC + SSD_HEADS + S5_WIDTH + RG_WIDTH + RG_WIDTH


def layer_norm_2(x, g, b):
    x32 = x.astype(jnp.float32)
    mu = jnp.mean(x32, axis=-1, keepdims=True)
    var = jnp.mean(jnp.square(x32 - mu), axis=-1, keepdims=True)
    return (x32 - mu) * lax.rsqrt(var + LN_EPS) * g.astype(jnp.float32) + b.astype(jnp.float32)

def causal_dwconv(x, w, b):
    k, c = w.shape
    y = lax.conv_general_dilated(x, w[:, None, :].astype(x.dtype), window_strides=(1,),
                                 padding=[(k - 1, 0)], dimension_numbers=('NWC', 'WIO', 'NWC'),
                                 feature_group_count=c)
    return y + b.astype(x.dtype)

def _lin_combine(left, right):
    a1, b1 = left
    a2, b2 = right
    return a1 * a2, a2 * b1 + b2

def linear_scan(a, b):
    return lax.associative_scan(_lin_combine, (a, b), axis=1)[1]

def ssd_mixer(z, xbc, dt_raw, conv_w, conv_b, dt_bias, a_log, d_skip, norm_w):
    bsz, seq, _ = z.shape
    nc = seq // SSD_CHUNK
    xbc = jax.nn.silu(causal_dwconv(xbc, conv_w.astype(jnp.float32), conv_b.astype(jnp.float32)))
    xs = xbc[..., :SSD_WIDTH]
    bm = xbc[..., SSD_WIDTH:SSD_WIDTH + SSD_GROUPS * SSD_STATE]
    cm = xbc[..., SSD_WIDTH + SSD_GROUPS * SSD_STATE:]
    dt = jax.nn.softplus(dt_raw + dt_bias.astype(jnp.float32))
    a = -jnp.exp(a_log.astype(jnp.float32))
    g, hg, p, n, q = SSD_GROUPS, SSD_HEADS_PER_GROUP, SSD_HEAD_DIM, SSD_STATE, SSD_CHUNK
    xh = xs.reshape(bsz, seq, SSD_HEADS, p)
    xdt = (xh * dt[..., None]).reshape(bsz, nc, q, g, hg, p)
    adt = (dt * a).reshape(bsz, nc, q, g, hg).transpose(0, 1, 3, 4, 2)
    bc = bm.reshape(bsz, nc, q, g, n)
    cc = cm.reshape(bsz, nc, q, g, n)
    a_cs = jnp.cumsum(adt, axis=-1)
    mask = jnp.tril(jnp.ones((q, q), dtype=bool))
    seg = a_cs[..., :, None] - a_cs[..., None, :]
    lmat = jnp.exp(jnp.where(mask, seg, -jnp.inf))
    cb = jnp.einsum('bclgn,bcsgn->bcgls', cc, bc)
    y_diag = jnp.einsum('bcgls,bcghls,bcsghp->bclghp', cb, lmat, xdt)
    decay_states = jnp.exp(a_cs[..., -1:] - a_cs)
    states = jnp.einsum('bclgn,bcghl,bclghp->bcghpn', bc, decay_states, xdt)
    chunk_decay = jnp.exp(a_cs[..., -1])

    def step(s, inp):
        st, dec = inp
        return s * dec[..., None, None] + st, s

    init = jnp.zeros((bsz, g, hg, p, n), jnp.float32)
    _, prev = lax.scan(step, init, (jnp.moveaxis(states, 1, 0), jnp.moveaxis(chunk_decay, 1, 0)))
    prev = jnp.moveaxis(prev, 0, 1)
    y_off = jnp.einsum('bclgn,bcghpn,bcghl->bclghp', cc, prev, jnp.exp(a_cs))
    y = (y_diag + y_off).reshape(bsz, seq, SSD_HEADS, p) + xh * d_skip.astype(jnp.float32)[:, None]
    y = y.reshape(bsz, seq, SSD_WIDTH) * jax.nn.silu(z)
    y = y * lax.rsqrt(jnp.mean(jnp.square(y), axis=-1, keepdims=True) + LN_EPS)
    return y * norm_w.astype(jnp.float32)

def s5_mixer(u, lam_re, lam_im, log_step, b_re, b_im, c_re, c_im, d_skip, glu_w, glu_b):
    bsz, seq, _ = u.shape
    f32 = jnp.float32
    ug = u.reshape(bsz, seq, S5_GROUPS, S5_GROUP_CH).astype(jnp.complex64)
    lam = lax.complex(lam_re.astype(f32), lam_im.astype(f32))
    step = jnp.exp(log_step.astype(f32))[:, None]
    lam_bar = jnp.exp(lam * step)
    bmat = lax.complex(b_re.astype(f32), b_im.astype(f32))
    b_bar = ((lam_bar - 1.0) / lam)[..., None] * bmat
    bu = jnp.einsum('gpc,blgc->blgp', b_bar, ug)
    h = linear_scan(jnp.broadcast_to(lam_bar, bu.shape), bu)
    cmat = lax.complex(c_re.astype(f32), c_im.astype(f32))
    y = jnp.real(jnp.einsum('gcp,blgp->blgc', cmat, h)).reshape(bsz, seq, S5_WIDTH)
    y = jax.nn.gelu(y + d_skip.astype(f32) * u)
    return y * jax.nn.sigmoid(jnp.einsum('blc,ce->ble', y, glu_w.astype(f32)) + glu_b.astype(f32))

def rglru_mixer(xr, gate_in, conv_w, conv_b, wa, ba, wx, bx, lam):
    bsz, seq, _ = xr.shape
    f32 = jnp.float32
    xc = causal_dwconv(xr, conv_w.astype(f32), conv_b.astype(f32))
    xh = xc.reshape(bsz, seq, RG_BLOCKS, RG_BLOCK_DIM)
    r = jax.nn.sigmoid(jnp.einsum('blhi,hij->blhj', xh, wa.astype(f32)) + ba.astype(f32)).reshape(bsz, seq, RG_WIDTH)
    i = jax.nn.sigmoid(jnp.einsum('blhi,hij->blhj', xh, wx.astype(f32)) + bx.astype(f32)).reshape(bsz, seq, RG_WIDTH)
    log_a = -RG_C * r * jax.nn.softplus(-lam.astype(f32))
    a = jnp.exp(log_a)
    mult = jnp.sqrt(-jnp.expm1(2.0 * log_a))
    h = linear_scan(a, mult * (i * xc))
    return h * jax.nn.gelu(gate_in)

def cross_attention(x, mem, wq, wk, wv, wo):
    bsz, seq, _ = x.shape
    f32 = jnp.float32
    q = jnp.einsum('bld,de->ble', x, wq.astype(f32)).reshape(bsz, seq, XA_HEADS, XA_HEAD_DIM)
    k = jnp.einsum('bmd,de->bme', mem, wk.astype(f32)).reshape(bsz, -1, XA_HEADS, XA_HEAD_DIM)
    v = jnp.einsum('bmd,de->bme', mem, wv.astype(f32)).reshape(bsz, -1, XA_HEADS, XA_HEAD_DIM)
    s = jnp.einsum('blhd,bmhd->bhlm', q, k) * (1.0 / math.sqrt(XA_HEAD_DIM))
    pr = jax.nn.softmax(s, axis=-1)
    o = jnp.einsum('bhlm,bmhd->blhd', pr, v).reshape(bsz, seq, D_MODEL)
    return jnp.einsum('ble,ed->bld', o, wo.astype(f32))

def squared_relu_mlp(x, w1, w2):
    hdn = jnp.square(jax.nn.relu(jnp.einsum('bld,df->blf', x, w1.astype(jnp.float32))))
    return jnp.einsum('blf,fd->bld', hdn, w2.astype(jnp.float32))

def second_inputs(seed: int = 0) -> dict:
    key = jax.random.key(seed)
    ks = iter(jax.random.split(key, 64))
    f32 = jnp.float32

    def nrm(shape, scale):
        return jax.random.normal(next(ks), shape, f32) * scale

    def uni(shape, lo, hi):
        return jax.random.uniform(next(ks), shape, f32, lo, hi)

    L = DEPTH
    x = nrm((BATCH, SEQ, D_MODEL), 1.0)
    mem = nrm((BATCH, MEM_LEN, D_MODEL), 1.0)
    dt0 = jnp.exp(uni((L, SSD_HEADS), math.log(1e-3), math.log(1e-1)))
    a_rg = uni((L, RG_WIDTH), 0.9, 0.999) ** (1.0 / RG_C)
    n_idx = jnp.arange(S5_STATE, dtype=f32)
    return {
        "x": x,
        "mem": mem,
        "w_in": nrm((L, D_MODEL, D_IN_2), D_MODEL ** -0.5),
        "w_out": nrm((L, D_MIX_2, D_MODEL), BETA * D_MIX_2 ** -0.5),
        "ssd_conv_w": nrm((L, SSD_CONV, SSD_XBC), SSD_CONV ** -0.5),
        "ssd_conv_b": nrm((L, SSD_XBC), 0.02),
        "ssd_dt_bias": dt0 + jnp.log(-jnp.expm1(-dt0)),
        "ssd_a_log": jnp.log(uni((L, SSD_HEADS), 1.0, 16.0)),
        "ssd_d": 1.0 + nrm((L, SSD_HEADS), 0.02),
        "ssd_norm_w": 1.0 + nrm((L, SSD_WIDTH), 0.02),
        "s5_lam_re": -0.5 + nrm((L, S5_GROUPS, S5_STATE), 0.01),
        "s5_lam_im": jnp.pi * n_idx + nrm((L, S5_GROUPS, S5_STATE), 0.01),
        "s5_log_step": uni((L, S5_GROUPS), math.log(1e-3), math.log(1e-1)),
        "s5_b_re": nrm((L, S5_GROUPS, S5_STATE, S5_GROUP_CH), (2.0 * S5_GROUP_CH) ** -0.5),
        "s5_b_im": nrm((L, S5_GROUPS, S5_STATE, S5_GROUP_CH), (2.0 * S5_GROUP_CH) ** -0.5),
        "s5_c_re": nrm((L, S5_GROUPS, S5_GROUP_CH, S5_STATE), (2.0 * S5_STATE) ** -0.5),
        "s5_c_im": nrm((L, S5_GROUPS, S5_GROUP_CH, S5_STATE), (2.0 * S5_STATE) ** -0.5),
        "s5_d": nrm((L, S5_WIDTH), 1.0),
        "s5_glu_w": nrm((L, S5_WIDTH, S5_WIDTH), S5_WIDTH ** -0.5),
        "s5_glu_b": nrm((L, S5_WIDTH), 0.02),
        "rg_conv_w": nrm((L, RG_CONV, RG_WIDTH), RG_CONV ** -0.5),
        "rg_conv_b": nrm((L, RG_WIDTH), 0.02),
        "rg_wa": nrm((L, RG_BLOCKS, RG_BLOCK_DIM, RG_BLOCK_DIM), RG_BLOCK_DIM ** -0.5),
        "rg_ba": nrm((L, RG_BLOCKS, RG_BLOCK_DIM), 0.02),
        "rg_wx": nrm((L, RG_BLOCKS, RG_BLOCK_DIM, RG_BLOCK_DIM), RG_BLOCK_DIM ** -0.5),
        "rg_bx": nrm((L, RG_BLOCKS, RG_BLOCK_DIM), 0.02),
        "rg_lambda": jnp.log(a_rg / (1.0 - a_rg)),
        "ln1_g": 1.0 + nrm((L, D_MODEL), 0.02),
        "ln1_b": nrm((L, D_MODEL), 0.02),
        "xa_wq": nrm((L, D_MODEL, D_MODEL), D_MODEL ** -0.5),
        "xa_wk": nrm((L, D_MODEL, D_MODEL), D_MODEL ** -0.5),
        "xa_wv": nrm((L, D_MODEL, D_MODEL), BETA * D_MODEL ** -0.5),
        "xa_wo": nrm((L, D_MODEL, D_MODEL), BETA * D_MODEL ** -0.5),
        "ln2_g": 1.0 + nrm((L, D_MODEL), 0.02),
        "ln2_b": nrm((L, D_MODEL), 0.02),
        "mlp_w1": nrm((L, D_MODEL, D_FF_2), BETA * D_MODEL ** -0.5),
        "mlp_w2": nrm((L, D_FF_2, D_MODEL), BETA * D_FF_2 ** -0.5),
        "ln3_g": 1.0 + nrm((L, D_MODEL), 0.02),
        "ln3_b": nrm((L, D_MODEL), 0.02),
    }

def second_block(x, mem, w_in, w_out, ssd_conv_w, ssd_conv_b, ssd_dt_bias, ssd_a_log, ssd_d, ssd_norm_w,
              s5_lam_re, s5_lam_im, s5_log_step, s5_b_re, s5_b_im, s5_c_re, s5_c_im, s5_d, s5_glu_w, s5_glu_b,
              rg_conv_w, rg_conv_b, rg_wa, rg_ba, rg_wx, rg_bx, rg_lambda, ln1_g, ln1_b,
              xa_wq, xa_wk, xa_wv, xa_wo, ln2_g, ln2_b, mlp_w1, mlp_w2, ln3_g, ln3_b):
    f32 = jnp.float32
    out_dtype = x.dtype
    h = x.astype(f32)
    memf = mem.astype(f32)
    split_idx = []
    acc = 0
    for w in IN_COLS[:-1]:
        acc += w
        split_idx.append(acc)
    for l in range(DEPTH):
        proj = jnp.einsum('bld,dk->blk', h, w_in[l].astype(f32))
        z, xbc, dt_raw, u_s5, x_rg, g_rg = jnp.split(proj, split_idx, axis=-1)
        y_ssd = ssd_mixer(z, xbc, dt_raw, ssd_conv_w[l], ssd_conv_b[l], ssd_dt_bias[l], ssd_a_log[l],
                          ssd_d[l], ssd_norm_w[l])
        y_s5 = s5_mixer(u_s5, s5_lam_re[l], s5_lam_im[l], s5_log_step[l], s5_b_re[l], s5_b_im[l],
                        s5_c_re[l], s5_c_im[l], s5_d[l], s5_glu_w[l], s5_glu_b[l])
        y_rg = rglru_mixer(x_rg, g_rg, rg_conv_w[l], rg_conv_b[l], rg_wa[l], rg_ba[l], rg_wx[l], rg_bx[l],
                           rg_lambda[l])
        y = jnp.concatenate([y_ssd, y_s5, y_rg], axis=-1)
        y = jnp.einsum('ble,ed->bld', y, w_out[l].astype(f32))
        h = layer_norm_2(ALPHA * h + y, ln1_g[l], ln1_b[l])
        h = layer_norm_2(ALPHA * h + cross_attention(h, memf, xa_wq[l], xa_wk[l], xa_wv[l], xa_wo[l]),
                       ln2_g[l], ln2_b[l])
        h = layer_norm_2(ALPHA * h + squared_relu_mlp(h, mlp_w1[l], mlp_w2[l]), ln3_g[l], ln3_b[l])
    return h.astype(out_dtype)


_first_inputs_2 = second_inputs


def second_inputs(seed=0):
    import zlib

    import numpy as np

    out = dict(_first_inputs_2(seed))
    spreads = {}
    factors = {'ssd_conv_b': 5.171,
     'ssd_d': 8.0,
     'ssd_norm_w': 23.274,
     's5_lam_re': 64.0,
     's5_lam_im': 64.0,
     's5_log_step': 64.0,
     's5_b_re': 64.0,
     's5_b_im': 64.0,
     's5_c_re': 64.0,
     's5_c_im': 64.0,
     's5_glu_b': 200.0,
     'rg_conv_b': 94.76,
     'rg_ba': 200.0,
     'rg_bx': 200.0,
     'ln1_g': 25.983,
     'ln1_b': 22.987,
     'ln2_g': 7.718,
     'ln2_b': 7.781,
     'ln3_g': 20.343,
     'ln3_b': 21.427,
     's5_glu_w': 43.507,
     'rg_wa': 38.392,
     'rg_wx': 21.848,
     'rg_lambda': 32.32,
     's5_d': 4.242,
     'rg_conv_w': 8.0}
    for name, (base, spread) in spreads.items():
        noise = np.random.default_rng([zlib.crc32(name.encode()), seed]).standard_normal(out[name].shape)
        drawn = base * np.exp(spread * noise) if base else spread * noise
        out[name] = __import__('jax').numpy.asarray(drawn.astype(out[name].dtype))
    for name, factor in factors.items():
        out[name] = (out[name] * factor).astype(out[name].dtype)
    return out


_narrow_inputs_2 = second_inputs


def second_inputs(seed=0):
    out = dict(_narrow_inputs_2(seed))
    wider = {'mem': 5.27,
     's5_glu_b': 9.67,
     'ln1_g': 3.14,
     'ln1_b': 3.15,
     'xa_wq': 5.26,
     'xa_wk': 5.26,
     'xa_wv': 5.23,
     'xa_wo': 5.26,
     'ln3_g': 3.07,
     'ln3_b': 3.07}
    for name, times in wider.items():
        mean = out[name].mean()
        out[name] = (mean + times * (out[name] - mean)).astype(out[name].dtype)
    return out


def setup_inputs(seed=0):
    out = dict(first_inputs(seed))
    for name, value in second_inputs(seed + 1).items():
        if name != "x":
            out[name + "_2"] = value
    return out


def reference(
    x, p, norm_mix_g, w_in, gmlp_v_g, gmlp_v_b, gmlp_w_s, gmlp_b_s, dn_conv_w, dn_a_log,
    dn_dt_bias, dn_o_g, rw_mu, rw_w0, rw_w2, rw_a0, rw_a2, rw_g2, rw_k_k, rw_k_a, rw_r_k,
    rw_lnx_g, rw_lnx_b, cf_conv_w, cf_conv_b, cf_ln_g, cf_ln_b, w_out, norm_ffn_g, w_ffn_gate,
    w_ffn_up, ffn_conv_w, w_ffn_down, norm_ple_g, w_ple_gate, w_ple_proj, final_norm_g, mem_2,
    w_in_2, w_out_2, ssd_conv_w_2, ssd_conv_b_2, ssd_dt_bias_2, ssd_a_log_2, ssd_d_2,
    ssd_norm_w_2, s5_lam_re_2, s5_lam_im_2, s5_log_step_2, s5_b_re_2, s5_b_im_2, s5_c_re_2,
    s5_c_im_2, s5_d_2, s5_glu_w_2, s5_glu_b_2, rg_conv_w_2, rg_conv_b_2, rg_wa_2, rg_ba_2,
    rg_wx_2, rg_bx_2, rg_lambda_2, ln1_g_2, ln1_b_2, xa_wq_2, xa_wk_2, xa_wv_2, xa_wo_2,
    ln2_g_2, ln2_b_2, mlp_w1_2, mlp_w2_2, ln3_g_2, ln3_b_2,
):
    x = first_block(
        x, p, norm_mix_g, w_in, gmlp_v_g, gmlp_v_b, gmlp_w_s, gmlp_b_s, dn_conv_w, dn_a_log,
        dn_dt_bias, dn_o_g, rw_mu, rw_w0, rw_w2, rw_a0, rw_a2, rw_g2, rw_k_k, rw_k_a, rw_r_k,
        rw_lnx_g, rw_lnx_b, cf_conv_w, cf_conv_b, cf_ln_g, cf_ln_b, w_out, norm_ffn_g,
        w_ffn_gate, w_ffn_up, ffn_conv_w, w_ffn_down, norm_ple_g, w_ple_gate, w_ple_proj,
        final_norm_g,
    )
    return second_block(
        x, mem_2, w_in_2, w_out_2, ssd_conv_w_2, ssd_conv_b_2, ssd_dt_bias_2, ssd_a_log_2,
        ssd_d_2, ssd_norm_w_2, s5_lam_re_2, s5_lam_im_2, s5_log_step_2, s5_b_re_2, s5_b_im_2,
        s5_c_re_2, s5_c_im_2, s5_d_2, s5_glu_w_2, s5_glu_b_2, rg_conv_w_2, rg_conv_b_2, rg_wa_2,
        rg_ba_2, rg_wx_2, rg_bx_2, rg_lambda_2, ln1_g_2, ln1_b_2, xa_wq_2, xa_wk_2, xa_wv_2,
        xa_wo_2, ln2_g_2, ln2_b_2, mlp_w1_2, mlp_w2_2, ln3_g_2, ln3_b_2,
    )


_drawn_inputs = setup_inputs


def setup_inputs(seed=0):
    import zlib

    import numpy as np

    out = dict(_drawn_inputs(seed))
    spreads = {}
    factors = {}
    for name, (base, spread) in spreads.items():
        noise = np.random.default_rng([zlib.crc32(name.encode()), seed]).standard_normal(out[name].shape)
        drawn = base * np.exp(spread * noise) if base else spread * noise
        out[name] = jnp.asarray(drawn.astype(out[name].dtype))
    for name, factor in factors.items():
        out[name] = (out[name] * factor).astype(out[name].dtype)
    return out
```

```python
from contextlib import ExitStack, contextmanager

import concourse.bass as bass
from concourse import mybir

ALU = mybir.AluOpType
ACT = mybir.ActivationFunctionType
F32 = mybir.dt.float32
AX_X = mybir.AxisListType.X

P = 128
T = 1024
BANK = 512
D = 1024
KD = D // P
NC = T // P
HEADS = 4
HD = 64
UNIT_K = 8
UNIT_M = 256
SLOTS = 4
LEVELS = 7

H0, N0, O0, R0, W0 = 0, 8, 16, 24, 40
TILES = 48


class Env:

    def tile(self, i, a=0, b=T):
        return self.arena[:, i * T + a:i * T + b]

    def words(self, i, offset, n):
        return self.arena[:, i * T + offset:i * T + offset + n]

    def col(self, name, k=0):
        j = self.cols_at[name] + k
        return self.cols[:, j:j + 1]

    def ps(self, a, b):
        return self.psum[:, a:b]


@contextmanager
def stage(env, *names):
    nc = env.nc
    sems = [nc.alloc_semaphore(f"{n}_{env.stages}") for n in names]
    env.stages += 1
    with nc.Block() as block:
        yield (block, *sems)
    for s in sems:
        nc.gpsimd.sem_clear(s)
    nc.all_engine_barrier()
    for s in sems:
        nc.release_semaphore(s)


def fin(eng, ins, sem, value):
    ins.then_inc(sem, 1)
    eng.wait_ge(sem, value)


def rep(ap, n):
    return ap.unsqueeze(1).broadcast_to([ap.shape[0], n, ap.shape[1]])



def gemm_stage(env, parts, x0, kt, groups, consumers, extra=(), start_with=(),
               product=None, aside=None):
    nc = env.nc
    nkb = -(-kt // UNIT_K)
    np_ = len(parts)
    per_group = np_ * nkb
    views = [w.rearrange("(k p) m -> p k m", p=P) for w in parts]
    period = 1
    while (period * per_group) % SLOTS or (np_ == 1 and period % 2):
        period += 1
    loops = groups // period if groups // period > 1 else 0
    u0 = env.units

    with stage(env, "set0_free", "set1_free", *extra) as (block, set0_free, set1_free, *more):
        set_free = [set0_free, set1_free]

        def each_group(eng, body):
            if loops:
                with eng.Fori(0, loops) as it:
                    for j in range(period):
                        body(it * period + j, j, it)
            for g in range(loops * period, groups):
                body(g, g % period, None)

        def unit(g, j, it, p, kb):
            if it is None:
                u = u0 + g * per_group + p * nkb + kb
                return u, u % SLOTS, u // SLOTS + 1
            u = u0 + j * per_group + p * nkb + kb
            return u + it * (period * per_group), u % SLOTS, it * (period * per_group // SLOTS) + (u // SLOTS + 1)

        @block.sync
        def _(sp):
            def load(g, j, it):
                for p in range(np_):
                    for kb in range(nkb):
                        u, slot, fills = unit(g, j, it, p, kb)
                        nk = min(UNIT_K, kt - kb * UNIT_K)
                        if it is not None or u >= SLOTS:
                            sp.wait_ge(env.unit_done, u - (SLOTS - 1))
                        dst = env.wslot(slot).rearrange("p (k m) -> p k m", m=UNIT_M)[:, 0:nk, :]
                        sp.dma_start(dst, views[p][:, kb * UNIT_K:kb * UNIT_K + nk, bass.ds(g * UNIT_M, UNIT_M)]
                                     ).then_inc(env.w_in[slot], 16)
            if u0 < SLOTS and loops:
                raise AssertionError("the first products must not loop: their first waits are left out")
            each_group(sp, load)

        @block.tensor
        def _(pe):
            def products(g, j, it):
                for p in range(np_):
                    s = p if np_ == 2 else j % 2
                    for kb in range(nkb):
                        u, slot, fills = unit(g, j, it, p, kb)
                        nk = min(UNIT_K, kt - kb * UNIT_K)
                        pe.wait_ge(env.w_in[slot], fills * 16)
                        if kb == 0:
                            turn = g if np_ == 2 else (g // 2 if it is None else it * (period // 2) + j // 2)
                            pe.wait_ge(set_free[s], turn + 1)
                        w = env.wslot(slot).rearrange("p (k m) -> p k m", m=UNIT_M)
                        if product:
                            product(w, s).then_inc(env.unit_done, 1)
                            continue
                        for m in range(2):
                            for k in range(nk):
                                kk = kb * UNIT_K + k
                                for n in range(2):
                                    c = s * 4 * BANK + m * T + n * BANK
                                    mm = nc.tensor.matmul(env.ps(c, c + BANK), w[:, k, m * P:(m + 1) * P],
                                                          env.tile(x0 + kk, n * BANK, (n + 1) * BANK),
                                                          start=(kk == 0), stop=(kk == kt - 1))
                        mm.then_inc(env.unit_done, 1)
            for s in range(2):
                pe.sem_inc(set_free[s], 1)
            for name in start_with:
                pe.sem_inc(more[extra.index(name)], 1)
            each_group(pe, products)

        def consume(eng, f):
            def one(g, j, it):
                def wait(p):
                    u = unit(g, j, it, p, nkb - 1)[0]
                    eng.wait_ge(env.unit_done, u + 1)
                    return g // 2 if it is None else it * (period // 2) + j // 2
                half = j % 2 if np_ == 1 else None
                f(eng, g, half, wait, lambda ins, p: ins.then_inc(set_free[p if np_ == 2 else j % 2], 1), [*more, *set_free])
            each_group(eng, one)

        if "scalar" in consumers:
            @block.scalar
            def _(act):
                consume(act, consumers["scalar"])
        if aside:
            @block.vector
            def _(dve):
                aside(dve, more)
        if "vector" in consumers:
            @block.vector
            def _(dve):
                consume(dve, consumers["vector"])
    env.units += groups * per_group



def norm_stage(env, groups, ones, inv_n, eps, scratch, center=False, post=None):
    nc = env.nc
    sq = (scratch, scratch + 1)
    rstd = scratch + 2
    total = sum(len(g[0]) for g in groups)
    with stage(env, "sum_done", "centred", "sq_ready", "sq_used", "std_ready", "inv_ready", "scaled") as (
            block, sum_done, centred, sq_ready, sq_used, std_ready, inv_ready, scaled):

        @block.tensor
        def _(pe):
            n_sq = 0
            for gi, (src, dst, gains) in enumerate(groups):
                base = (gi % 2) * 4 * BANK
                if gi >= 2:
                    pe.wait_ge(std_ready, gi - 1)
                if center:
                    for i, t in enumerate(src):
                        for n in range(2):
                            mm = nc.tensor.matmul(env.ps(base + n * BANK, base + (n + 1) * BANK), ones,
                                                  env.tile(t, n * BANK, (n + 1) * BANK),
                                                  start=(i == 0), stop=(i == len(src) - 1))
                    mm.then_inc(sum_done, 1)
                for i in range(len(src)):
                    pe.wait_ge(sq_ready, n_sq + 1)
                    for n in range(2):
                        c = base + T + n * BANK
                        mm = nc.tensor.matmul(env.ps(c, c + BANK), ones, env.tile(sq[n_sq % 2], n * BANK, (n + 1) * BANK),
                                              start=(i == 0), stop=(i == len(src) - 1))
                    mm.then_inc(sq_used, 1)
                    n_sq += 1

        @block.vector
        def _(dve):
            done = 0
            n_centred = 0
            for gi, (src, dst, gains) in enumerate(groups):
                base = (gi % 2) * 4 * BANK
                if center:
                    dve.wait_ge(sum_done, gi + 1)
                    for s, d in zip(src, dst):
                        n_centred += 1
                        nc.vector.scalar_tensor_tensor(env.tile(d), env.ps(base, base + T), -inv_n, env.tile(s),
                                                       ALU.mult, ALU.add).then_inc(centred, 1)
                    dve.wait_ge(centred, n_centred)
                dve.wait_ge(std_ready, gi + 1)
                fin(dve, nc.vector.reciprocal(env.tile(rstd), env.tile(rstd)), inv_ready, gi + 1)
                for i, (s, d) in enumerate(zip(src, dst)):
                    gain = gains[i] if gains else 1.0
                    nc.vector.scalar_tensor_tensor(env.tile(d), env.tile(d if center else s), gain, env.tile(rstd),
                                                   ALU.mult, ALU.mult).then_inc(scaled, 1)

        @block.scalar
        def _(act):
            n_sq = 0
            for gi, (src, dst, gains) in enumerate(groups):
                base = (gi % 2) * 4 * BANK
                before = n_sq
                for s, d in zip(src, dst):
                    if center:
                        act.wait_ge(centred, n_sq + 1)
                    if n_sq >= 2:
                        act.wait_ge(sq_used, n_sq - 1)
                    nc.scalar.activation(env.tile(sq[n_sq % 2]), env.tile(d if center else s), ACT.Square
                                         ).then_inc(sq_ready, 1)
                    n_sq += 1
                act.wait_ge(sq_used, n_sq)
                if gi:
                    act.wait_ge(scaled, before)
                nc.scalar.activation(env.tile(rstd), env.ps(base + T, base + 2 * T), ACT.Sqrt, scale=inv_n,
                                     bias=env.col(eps)).then_inc(std_ready, 1)
            if post:
                n = 0
                for gi, (src, dst, gains) in enumerate(groups):
                    for i, d in enumerate(dst):
                        n += 1
                        act.wait_ge(scaled, n)
                        func, bias = post(gi, i)
                        nc.scalar.activation(env.tile(d), env.tile(d), func, bias=bias)


def conv_stage(env, jobs, taps, func=None):
    nc = env.nc
    with stage(env, "first_ready", "tap_done", "conv_done") as (block, first_ready, tap_done, conv_done):
        @block.scalar
        def _(act):
            for i, (s, d, w, bias) in enumerate(jobs):
                nc.scalar.activation(env.tile(d), env.tile(s), ACT.Identity, scale=w[taps - 1], bias=bias
                                     ).then_inc(first_ready, 1)
            if func is not None:
                for i, (s, d, w, bias) in enumerate(jobs):
                    act.wait_ge(conv_done, i + 1)
                    nc.scalar.activation(env.tile(d), env.tile(d), func)

        @block.vector
        def _(dve):
            n = 0
            for i, (s, d, w, bias) in enumerate(jobs):
                dve.wait_ge(first_ready, i + 1)
                for back in range(1, taps):
                    ins = nc.vector.scalar_tensor_tensor(env.tile(d, back), env.tile(s, 0, T - back), w[taps - 1 - back],
                                                         env.tile(d, back), ALU.mult, ALU.add)
                    if back == taps - 1:
                        ins.then_inc(conv_done, 1)
                    else:
                        n += 1
                        fin(dve, ins, tap_done, n)


def token_major_stage(env, srcs, dst):
    nc = env.nc
    w = len(srcs) * P
    per_bank = BANK // P
    n_banks = len(srcs) * NC // per_bank
    pairs = [(c, i) for c in range(NC) for i in range(len(srcs))]
    with stage(env, "turned", "copied") as (block, turned, copied):
        @block.tensor
        def _(pe):
            for b in range(n_banks):
                if b >= 8:
                    pe.wait_ge(copied, b - 7)
                for q in range(per_bank):
                    c, i = pairs[b * per_bank + q]
                    col = (b % 8) * BANK + q * P
                    mm = nc.tensor.transpose(env.ps(col, col + P), env.tile(srcs[i], c * P, (c + 1) * P), env.const["ident"])
                mm.then_inc(turned, 1)

        @block.vector
        def _(dve):
            for b in range(n_banks):
                dve.wait_ge(turned, b + 1)
                nc.vector.tensor_copy(env.words(dst, b * BANK, BANK), env.ps((b % 8) * BANK, (b % 8 + 1) * BANK)
                                      ).then_inc(copied, 1)



def first_norm_and_gmlp(env):
    nc, dr = env.nc, env.dram
    norm_stage(env, [(range(H0, H0 + KD), range(N0, N0 + KD), [env.col("norm_mix_g", k) for k in range(KD)])],
               env.const["ones"], 1.0 / D, "eps6", W0)

    u0, v0, vt0, ws0 = R0, R0 + 2, R0 + 4, R0 + 6

    def gelu(act, g, half, wait, free, sems):
        wait(0)
        for m in range(2):
            c = half * 4 * BANK + m * T
            ins = nc.scalar.activation(env.tile(u0 + 2 * g + m), env.ps(c, c + T), ACT.Gelu_apprx_tanh)
        free(ins, 0)
    gemm_stage(env, [dr["w_in"][:, 0:512]], N0, KD, 2, {"scalar": gelu})
    norm_stage(env, [((v0, v0 + 1), (v0, v0 + 1), [env.col("gmlp_v_g", k) for k in range(2)])],
               env.const["ones"], 1.0 / 256, "eps5", W0, center=True,
               post=lambda gi, i: (ACT.Identity, env.col("gmlp_v_b", i)))
    token_major_stage(env, (v0, v0 + 1), vt0)

    w_s = env.words(ws0, 0, HEADS * P).rearrange("j (h i) -> j h i", h=HEADS)
    b_s = env.words(ws0 + 1, 0, HEADS * P)[0:1, :]
    with stage(env, "ws_in", "ws_ready", "mixed") as (block, ws_in, ws_ready, mixed):
        @block.sync
        def _(sp):
            sp.dma_start(w_s, dr["gmlp_w_sT"].rearrange("j (h i) -> j h i", h=HEADS)).then_inc(ws_in, 16)
            sp.dma_start(b_s, dr["gmlp_b_s"]).then_inc(ws_in, 16)

        @block.tensor
        def _(pe):
            pe.wait_ge(ws_ready, 1)
            for i in range(2):
                for b in range(NC):
                    for h in (2 * i, 2 * i + 1):
                        lo = (h % 2) * HD
                        c = i * T + b * P
                        out = env.psum[lo:lo + HD, c:c + P]
                        nc.tensor.matmul(out, env.words(vt0, b * 256 + h * HD, HD), w_s[:, h, :], start=True, stop=False)
                        mm = nc.tensor.matmul(out, env.const["ones"][0:1, 0:HD], b_s[:, h * P:(h + 1) * P], start=False, stop=True)
                mm.then_inc(mixed, 1)

        @block.vector
        def _(dve):
            dve.wait_ge(ws_in, 32)
            nc.vector.memset(w_s[HD:P, :, 0:HD], 0.0).then_inc(ws_ready, 1)
            for i in range(2):
                dve.wait_ge(mixed, i + 1)
                nc.vector.tensor_tensor(env.tile(O0 + i), env.tile(u0 + i), env.ps(i * T, (i + 1) * T), ALU.mult)



class Words:

    def __init__(self, env, regions):
        self.env, self.regions = env, [[t * T, t * T + n] for t, n in regions]

    def take(self, n):
        for r in self.regions:
            if r[1] - r[0] >= n:
                a = r[0]
                r[0] += n
                return self.env.arena[:, a:a + n]
        raise AssertionError("no room")


def softplus_stage(env, jobs):
    nc = env.nc
    with stage(env, "act_step", "logs") as (block, act_step, logs):
        @block.scalar
        def _(act):
            n = 0
            for src, dst, spare, scale, bias in jobs:
                rows = src.shape[0]
                fin(act, nc.scalar.activation(dst, src, ACT.Identity, scale=scale, bias=bias), act_step, n + 1)
                fin(act, nc.scalar.activation(spare, dst, ACT.Abs), act_step, n + 2)
                fin(act, nc.scalar.activation(spare, spare, ACT.Exp, scale=-1.0), act_step, n + 3)
                nc.scalar.activation(spare, spare, ACT.Ln, scale=1.0, bias=env.col("one")[0:rows]).then_inc(logs, 1)
                n += 3

        @block.vector
        def _(dve):
            for i, (src, dst, spare, scale, bias) in enumerate(jobs):
                dve.wait_ge(logs, i + 1)
                nc.vector.scalar_tensor_tensor(dst, dst, 0.0, spare, ALU.max, ALU.add)


def small_rows_gemm(env, w_dram, x0, jobs):
    nc = env.nc
    n = w_dram.shape[1]
    w = env.words(W0, 0, KD * n).rearrange("p (k m) -> p k m", m=n)
    with stage(env, "w_rows_in") as (block, w_rows_in):
        @block.sync
        def _(sp):
            sp.dma_start(w, w_dram.rearrange("(k p) m -> p k m", p=P)).then_inc(w_rows_in, 16)

        @block.tensor
        def _(pe):
            pe.wait_ge(w_rows_in, 16)
            for a, rows, c in jobs:
                for half in range(2):
                    for k in range(KD):
                        nc.tensor.matmul(env.psum[0:rows, c + half * BANK:c + (half + 1) * BANK], w[:, k, a:a + rows],
                                         env.tile(x0 + k, half * BANK, (half + 1) * BANK), start=(k == 0), stop=(k == KD - 1))


def chunk_sums(env, dve, dst, src, mask, sem, value):
    fin(dve, env.nc.vector.tensor_tensor_scan(dst, mask, src, 0.0, ALU.mult, ALU.add), sem, value)


def write_restart_mask(env, dve, mask, sem):
    fin(dve, env.nc.vector.memset(mask, 1.0), sem, 1)
    fin(dve, env.nc.vector.memset(mask.rearrange("p (c t) -> p c t", t=P)[:, :, 0:1], 0.0), sem, 2)


def by_head(ap, w):
    return ap.rearrange("p (h w) -> p h w", w=w)


def delta_chunks(env, room, kind, m):
    nc = env.nc
    rw = kind == "rwkv"
    tk = room.take
    names = ["aT", "lT", "rT", "kT"] if rw else ["aT", "lT", "rT", "kbT", "qd"]
    f = {n: tk(512 if n in ("lT", "kT") else 256) for n in names}
    tok = {n: tk(256) for n in (["v", "b", "k"] if rw else ["v", "b"])}
    lt, rb, xx, xt, vs = tk(512), tk(512), tk(512), tk(512), tk(512)
    ak, rk = (tk(512), tk(512)) if rw else (None, None)
    ee = None if rw else tk(512)
    ct = [tk(512), tk(512)]
    state = tk(256)
    rhs, us = vs[:, 0:256], vs[:, 256:512]
    bank = lambda b, n=BANK: env.ps(b * BANK, b * BANK + n)
    hp = lambda h: slice((h % 2) * HD, (h % 2) * HD + HD)
    fm = lambda ap, h: ap[:, (h // 2) * P:(h // 2 + 1) * P]
    sq = lambda ap, h: ap[:, h * P:(h + 1) * P]
    th = lambda ap, h: ap[:, h * HD:(h + 1) * HD]
    st = lambda h: state[:, h * HD:(h + 1) * HD]
    incl4, ident4 = rep(env.const["incl"], HEADS), rep(env.const["ident"], HEADS)
    nlev = LEVELS - 1
    pairs = ((0, (2, 3, 4)), (1, (5, 6, 7)))
    pw = lambda ap, p: ap[:, p * 2 * P:(p + 1) * 2 * P]

    def ftile(t0, it):
        return env.arena[:, t0 * T:(t0 + 2) * T].rearrange("p (i t) -> p i t", i=2)[:, :, bass.ds(it * P, P)]

    def tchunk(t0, it):
        return env.arena[:, t0 * T:(t0 + 2) * T][:, bass.ds(it * 256, 256)]

    with stage(env, "prep_ready", "diff_ready", "exp_ready", "gram_done", "lt_ready", "x0_ready", "turned", "ct_ready",
               "v_done", "vs_ready", "d_done", "x_ready", "p1_done", "rhs_ready", "u_done", "us_ready", "chunk_done",
               "s_ready", "dve_step") as (
            block, prep_ready, diff_ready, exp_ready, gram_done, lt_ready, x0_ready, turned, ct_ready, v_done, vs_ready,
            d_done, x_ready, p1_done, rhs_ready, u_done, us_ready, chunk_done, s_ready, dve_step):

        @block.gpsimd
        def _(pool):
            two = lambda ap: ap.rearrange("p (i t) -> p i t", i=2)
            def padded(dst, t0, it):
                for e in range(2):
                    own = env.col(f"half{e}").unsqueeze(2).broadcast_to([P, 2, P])
                    nc.gpsimd.tensor_tensor(dst.rearrange("p (i e t) -> p i e t", i=2, e=2)[:, :, e, :], ftile(t0, it),
                                            own, ALU.mult)

            with pool.Fori(0, NC) as it:
                pool.wait_ge(chunk_done, it + 1)
                if rw:
                    padded(f["lT"], m["bT"], it)
                    padded(f["kT"], m["kT"], it)
                    for n in ("aT", "rT"):
                        nc.gpsimd.tensor_copy(two(f[n]), ftile(m[n], it))
                    nc.gpsimd.tensor_copy(tok["v"], tchunk(m["v_tok"], it))
                    nc.gpsimd.tensor_copy(tok["k"], tchunk(m["k_tok"], it))
                    nc.gpsimd.tensor_tensor(tok["b"], tchunk(m["b_tok"], it), env.col("minus_one").broadcast_to([P, 256]),
                                            ALU.mult).then_inc(prep_ready, 1)
                else:
                    padded(f["lT"], m["kT"], it)
                    nc.gpsimd.tensor_copy(two(f["rT"]), ftile(m["qT"], it))
                    nc.gpsimd.tensor_copy(two(f["kbT"]), ftile(m["kbT"], it))
                    nc.gpsimd.tensor_tensor(two(f["aT"]), ftile(m["kbT"], it), ftile(m["eg"], it), ALU.mult)
                    nc.gpsimd.tensor_tensor(two(f["qd"]), ftile(m["qT"], it), ftile(m["eg"], it), ALU.mult)
                    for n, src, scale in (("v", "v_tok", "beta_tok"), ("b", "k_tok", "kdec_tok")):
                        s = m[scale][:, bass.ds(it * HEADS, HEADS)].unsqueeze(2).broadcast_to([P, HEADS, HD])
                        ins = nc.gpsimd.tensor_tensor(by_head(tok[n], HD), by_head(tchunk(m[src], it), HD), s, ALU.mult)
                    ins.then_inc(prep_ready, 1)
                pool.wait_ge(lt_ready, it + 1)
                for lv in range(nlev):
                    if lv >= 2:
                        pool.wait_ge(v_done, it * (2 * nlev) + 2 * (lv - 1))
                    nc.gpsimd.tensor_tensor(by_head(ct[lv % 2], P), by_head(lt, P),
                                            rep(env.const[f"level{lv + 1}"], HEADS), ALU.mult).then_inc(ct_ready, 1)

        @block.tensor
        def _(pe):
            pe.sem_inc(chunk_done, 1)
            with pe.Fori(0, NC) as it:
                pe.wait_ge(prep_ready, it + 1)
                left = f["aT"] if rw else f["kbT"]
                grams = [(f["lT"], left, 0), (f["lT"], f["rT"], 1)]
                if rw:
                    grams += [(f["kT"], left, 5), (f["kT"], f["rT"], 6)]
                for a, b, bk in grams:
                    for h in range(HEADS):
                        mm = nc.tensor.matmul(sq(bank(bk), h), sq(a, h), fm(b, h), start=True, stop=True)
                mm.then_inc(gram_done, 1)
                pe.wait_ge(x0_ready, it + 1)
                for p, (bv, bd, bt) in pairs:
                    for e in range(2):
                        mm = nc.tensor.transpose(sq(bank(bv), e), sq(xt, 2 * p + e), env.const["ident"])
                    mm.then_inc(turned, 1)
                for lv in range(nlev):
                    last = lv == nlev - 1
                    pe.wait_ge(ct_ready, it * nlev + (lv + 1))
                    for p, (bv, bd, bt) in pairs:
                        pe.wait_ge(x_ready, it * (2 * nlev) + (2 * lv + p + 1))
                        for e in range(2):
                            h = 2 * p + e
                            mm = nc.tensor.matmul(sq(bank(bv), e), sq(ct[lv % 2], h), sq(xx, h), start=True, stop=True)
                        mm.then_inc(v_done, 1)
                    for p, (bv, bd, bt) in pairs:
                        pe.wait_ge(vs_ready, it * (2 * nlev) + (2 * lv + p + 1))
                        if not last:
                            for e in range(2):
                                nc.tensor.matmul(sq(bank(bd), e), sq(xt, 2 * p + e), sq(vs, 2 * p + e), start=True, stop=True)
                        for e in range(2):
                            mm = nc.tensor.matmul(sq(bank(bt), e), sq(vs, 2 * p + e), sq(xt, 2 * p + e), start=True, stop=True)
                        mm.then_inc(d_done, 1)
                pe.wait_ge(s_ready, it + 1)
                for h in range(HEADS):
                    mm = nc.tensor.matmul(th(bank(5), h), fm(f["aT"], h), st(h), start=True, stop=not rw)
                    if rw:
                        mm = nc.tensor.matmul(th(bank(5), h), sq(ak, h), th(tok["v"], h), start=False, stop=True)
                mm.then_inc(p1_done, 1)
                pe.wait_ge(rhs_ready, it + 1)
                for h in range(HEADS):
                    mm = nc.tensor.matmul(th(bank(6), h), sq(xt, h), th(rhs, h), start=True, stop=True)
                mm.then_inc(u_done, 1)
                pe.wait_ge(us_ready, it + 1)
                for h in range(HEADS):
                    o = env.psum[hp(h), 7 * BANK + (h // 2) * P:7 * BANK + (h // 2 + 1) * P]
                    nc.tensor.matmul(o, th(us, h), sq(rb, h), start=True, stop=False)
                    nc.tensor.matmul(o, st(h), fm(f["rT" if rw else "qd"], h), start=False, stop=not rw)
                    if rw:
                        nc.tensor.matmul(o, th(tok["v"], h), sq(rk, h), start=False, stop=True)
                for h in range(HEADS):
                    o = env.psum[hp(h), 3 * BANK + (h // 2) * HD:3 * BANK + (h // 2 + 1) * HD]
                    mm = nc.tensor.matmul(o, th(tok["b"], h), th(us, h), start=True, stop=not rw)
                    if rw:
                        mm = nc.tensor.matmul(o, th(tok["k"], h), th(tok["v"], h), start=False, stop=True)
                mm.then_inc(chunk_done, 1)

        @block.scalar
        def _(act):
            with act.Fori(0, NC) as it:
                if not rw:
                    act.wait_ge(diff_ready, it + 1)
                    nc.scalar.activation(ee, ee, ACT.Exp).then_inc(exp_ready, 1)
                for p, (bv, bd, bt) in pairs:
                    act.wait_ge(turned, it * 2 + (p + 1))
                    nc.scalar.activation(pw(xx, p), bank(bv, 256), ACT.Copy).then_inc(x_ready, 1)
                for lv in range(nlev):
                    for p, (bv, bd, bt) in pairs:
                        act.wait_ge(v_done, it * (2 * nlev) + (2 * lv + p + 1))
                        nc.scalar.activation(pw(vs, p), bank(bv, 256), ACT.Copy).then_inc(vs_ready, 1)
                act.wait_ge(u_done, it + 1)
                nc.scalar.activation(us, bank(6, 256), ACT.Copy).then_inc(us_ready, 1)
                act.wait_ge(chunk_done, it + 2)
                nc.scalar.activation(ftile(m["out"], it), bank(7, 256).rearrange("p (i t) -> p i t", i=2), ACT.Copy)

        @block.vector
        def _(dve):
            steps = 9 if rw else 5
            fin(dve, nc.vector.memset(state, 0.0), s_ready, 1)
            with dve.Fori(0, NC) as it:
                def step(ins, k):
                    fin(dve, ins, dve_step, it * steps + k)
                if not rw:
                    for h in range(HEADS):
                        g = env.arena[:, (m["g_rows"] + h) * T:(m["g_rows"] + h + 1) * T][:, bass.ds(it * P, P)]
                        ins = nc.vector.tensor_scalar(sq(ee, h), g, m["g_tok"][:, bass.ds(it * HEADS + h, 1)], 0.0,
                                                      ALU.subtract, ALU.min)
                    ins.then_inc(diff_ready, 1)
                    dve.wait_ge(exp_ready, it + 1)
                    step(nc.vector.tensor_tensor(by_head(ee, P), by_head(ee, P), incl4, ALU.mult), 1)
                    dve.wait_ge(gram_done, it + 1)
                    step(nc.vector.tensor_tensor(rb, bank(1), ee, ALU.mult), 2)
                    step(nc.vector.tensor_tensor(lt, bank(0), ee, ALU.mult), 3)
                else:
                    dve.wait_ge(gram_done, it + 1)
                    nc.vector.tensor_tensor(by_head(ak, P), by_head(bank(5), P), rep(env.const["strict"], HEADS), ALU.mult)
                    step(nc.vector.tensor_tensor(by_head(rk, P), by_head(bank(6), P), incl4, ALU.mult), 1)
                    step(nc.vector.scalar_tensor_tensor(by_head(rb, P), by_head(bank(1), P), -1.0, incl4, ALU.mult, ALU.mult), 2)
                    step(nc.vector.tensor_tensor(by_head(lt, P), by_head(bank(0), P), incl4, ALU.mult), 3)
                step(nc.vector.tensor_tensor(by_head(xt, P), by_head(lt, P), rep(env.const["level0"], HEADS), ALU.mult), 4)
                nc.vector.tensor_tensor(by_head(xt, P), ident4, by_head(xt, P), ALU.subtract).then_inc(x0_ready, 1)
                dve.sem_inc(lt_ready, 1)
                dve.wait_ge(x0_ready, it + 1)
                for lv in range(nlev):
                    for p, (bv, bd, bt) in pairs:
                        dve.wait_ge(d_done, it * (2 * nlev) + (2 * lv + p + 1))
                        if lv < nlev - 1:
                            nc.vector.tensor_tensor(pw(xx, p), pw(xx, p), bank(bd, 256), ALU.subtract)
                            nc.vector.tensor_tensor(pw(xt, p), pw(xt, p), bank(bt, 256), ALU.subtract).then_inc(x_ready, 1)
                        else:
                            last_x = nc.vector.tensor_tensor(pw(xt, p), pw(xt, p), bank(bt, 256), ALU.subtract)
                step(last_x, 5)
                dve.wait_ge(p1_done, it + 1)
                if rw:
                    nc.vector.tensor_copy(rhs, bank(5, 256)).then_inc(rhs_ready, 1)
                else:
                    nc.vector.tensor_tensor(rhs, tok["v"], bank(5, 256), ALU.subtract).then_inc(rhs_ready, 1)
                dve.wait_ge(chunk_done, it + 2)
                for h in range(HEADS):
                    i = h // 2
                    s = state[hp(h), h * HD:(h + 1) * HD]
                    ds = env.psum[hp(h), 3 * BANK + i * HD:3 * BANK + (i + 1) * HD]
                    decay = m["decay"](i, it)[hp(h)]
                    if rw:
                        step(nc.vector.tensor_tensor(s, s, ds, ALU.add), 6 + h)
                        ins = nc.vector.tensor_scalar(s, s, decay, None, ALU.mult)
                    else:
                        ins = nc.vector.scalar_tensor_tensor(s, s, decay, ds, ALU.mult, ALU.add)
                ins.then_inc(s_ready, 1)



def copies_to(env, t0, funcs):
    def f(act, g, half, wait, free, sems):
        wait(0)
        for m in range(2):
            c = half * 4 * BANK + m * T
            ins = env.nc.scalar.activation(env.tile(t0 + 2 * g + m), env.ps(c, c + T), funcs[g])
        free(ins, 0)
    return {"scalar": f}


def delta_net(env):
    nc, dr = env.nc, env.dram
    raw, gate, q, k, v = R0, R0 + 6, R0 + 8, R0 + 10, R0 + 12
    k_tok, v_tok, b_row, g_row = R0, R0 + 2, R0 + 4, R0 + 5
    kb, eg, g_rows, out = O0 + 4, W0, v, O0 + 2
    gemm_stage(env, [dr["w_in"][:, 512:1536]], N0, KD, 4, copies_to(env, raw, [ACT.Copy] * 3 + [ACT.Silu]),
               extra=("tap_done",), aside=lambda dve, sems: conformer_conv(env, dve, sems[0]))
    conformer_norm(env)
    conv_stage(env, [(raw + i, q + i, [env.col("dn_conv_w", 6 * j + i) for j in range(4)], 0.0) for i in range(6)], 4, ACT.Silu)
    norm_stage(env, [((q + i,), (q + i,), [HD ** -0.5]) for i in range(2)] + [((k + i,), (k + i,), None) for i in range(2)],
               env.const["ones64"], 1.0, "eps6", W0)
    token_major_stage(env, (k, k + 1), k_tok)
    token_major_stage(env, (v, v + 1), v_tok)

    small_rows_gemm(env, dr["w_in"][:, 1536:1544], N0, [(0, HEADS, 0), (HEADS, HEADS, T)])
    rows = lambda t: env.arena[0:HEADS, t * T:(t + 1) * T]
    alpha = rows(W0 + 1)
    softplus_stage(env, [(env.psum[0:HEADS, T:2 * T], alpha, rows(W0 + 2), 1.0, env.col("dn_dt_bias")[0:HEADS])])
    small = Words(env, [(W0 + 7, 512)])
    g_tok, beta_tok, kdec_tok = small.take(32), small.take(32), small.take(32)
    rate = small.take(1)[0:HEADS]
    with stage(env, "mask_step", "rate_ready", "g_step", "rows_ready") as (block, mask_step, rate_ready, g_step, rows_ready):
        @block.scalar
        def _(act):
            nc.scalar.activation(rate, env.col("dn_a_log")[0:HEADS], ACT.Exp).then_inc(rate_ready, 1)
            nc.scalar.activation(rows(b_row), env.psum[0:HEADS, 0:T], ACT.Sigmoid)

        @block.vector
        def _(dve):
            write_restart_mask(env, dve, rows(W0 + 2), mask_step)
            dve.wait_ge(rate_ready, 1)
            fin(dve, nc.vector.tensor_scalar(alpha, alpha, rate, -1.0, ALU.mult, ALU.mult), g_step, 1)
            chunk_sums(env, dve, rows(g_row), alpha, rows(W0 + 2), rows_ready, 1)

    sel = env.sel
    with stage(env, "spread", "spread2", "g_copied", "tok_copied", "kdec_step") as (
            block, spread, spread2, g_copied, tok_copied, kdec_step):
        @block.tensor
        def _(pe):
            for h in range(HEADS):
                for n in range(2):
                    mm = nc.tensor.matmul(env.ps(h * T + n * BANK, h * T + (n + 1) * BANK), sel[0:HEADS, h * P:(h + 1) * P],
                                          rows(g_row)[:, n * BANK:(n + 1) * BANK], start=True, stop=True)
                mm.then_inc(spread, 1)
            pe.wait_ge(g_copied, 4)
            for r, c0 in ((g_row, 0), (b_row, 2 * T)):
                for i in range(2):
                    for n in range(2):
                        c = c0 + i * T + n * BANK
                        mm = nc.tensor.matmul(env.ps(c, c + BANK), sel[0:HEADS, (4 + i) * P:(5 + i) * P],
                                              rows(r)[:, n * BANK:(n + 1) * BANK], start=True, stop=True)
                mm.then_inc(spread2, 1)
            pe.wait_ge(tok_copied, 2)
            for r, c0 in ((g_row, 0), (b_row, 32)):
                for c in range(NC):
                    mm = nc.tensor.matmul(env.ps(c0 + c * HEADS, c0 + (c + 1) * HEADS), rows(r)[:, c * P:(c + 1) * P],
                                          env.const["ident"][0:HEADS, 0:HEADS], start=True, stop=True)
            mm.then_inc(spread2, 1)

        @block.scalar
        def _(act):
            for h in range(HEADS):
                act.wait_ge(spread, h + 1)
                nc.scalar.activation(env.tile(g_rows + h), env.ps(h * T, (h + 1) * T), ACT.Copy).then_inc(g_copied, 1)
            act.wait_ge(spread2, 1)
            nc.scalar.activation(env.arena[:, eg * T:(eg + 2) * T], env.ps(0, 2 * T), ACT.Exp).then_inc(tok_copied, 1)
            act.wait_ge(kdec_step, 3)
            nc.scalar.activation(kdec_tok, kdec_tok, ACT.Exp)

        @block.vector
        def _(dve):
            dve.wait_ge(spread2, 2)
            nc.vector.tensor_tensor(env.arena[:, kb * T:(kb + 2) * T], env.arena[:, k * T:(k + 2) * T],
                                    env.ps(2 * T, 4 * T), ALU.mult).then_inc(tok_copied, 1)
            dve.wait_ge(spread2, 3)
            dve.wait_ge(g_copied, 4)
            fin(dve, nc.vector.tensor_copy(g_tok, env.ps(0, 32)), kdec_step, 1)
            nc.vector.tensor_copy(beta_tok, env.ps(32, 64)).then_inc(kdec_step, 1)
            last = env.arena[:, g_rows * T:(g_rows + HEADS) * T].rearrange("p (h c t) -> p c h t", h=HEADS, t=P)[:, :, :, P - 1]
            nc.vector.tensor_tensor(kdec_tok.rearrange("p (c h) -> p c h", h=HEADS), last,
                                    g_tok.rearrange("p (c h) -> p c h", h=HEADS), ALU.subtract).then_inc(kdec_step, 1)

    room = Words(env, [(W0 + 2, 5 * T), (R0 + 4, 2 * T)])
    delta_chunks(env, room, "dn", {
        "kT": k, "qT": q, "kbT": kb, "eg": eg, "v_tok": v_tok, "k_tok": k_tok, "beta_tok": beta_tok, "kdec_tok": kdec_tok,
        "g_rows": g_rows, "g_tok": g_tok, "out": out,
        "decay": lambda i, it: env.arena[:, (eg + i) * T:(eg + i + 1) * T][:, bass.ds(it * P + (P - 1), 1)]})
    norm_stage(env, [((out + i,), (out + i,), [env.col("dn_o_g")]) for i in range(2)], env.const["ones64"], 1.0 / HD, "eps6", W0)
    with stage(env) as (block,):
        @block.vector
        def _(dve):
            nc.vector.tensor_tensor(env.arena[:, out * T:(out + 2) * T], env.arena[:, out * T:(out + 2) * T],
                                    env.arena[:, gate * T:(gate + 2) * T], ALU.mult)


CF_H, CF_OUT = R0 + 8, O0 + 6
RWKV_RATE = float(2.718281828459045 ** -0.5)


def rwkv(env):
    nc, dr = env.nc, env.dram
    raw, mixed, out = R0, R0 + 8, O0 + 4
    r, k, v, xwa, xg = mixed, mixed + 2, mixed + 4, mixed + 6, mixed + 7
    lw, a, gate, kk = R0, R0 + 2, R0 + 4, R0 + 6
    gemm_stage(env, [dr["w_in"][:, 1544:2568]], N0, KD, 4, copies_to(env, raw, [ACT.Copy] * 4))

    with stage(env, "diff_step", "lora_in_ready") as (block, diff_step, lora_in_ready):
        @block.vector
        def _(dve):
            n = 0
            for i in range(8):
                d = env.tile(mixed + i)
                fin(dve, nc.vector.tensor_tensor(d[:, 1:T], env.tile(raw + i)[:, 0:T - 1], env.tile(raw + i)[:, 1:T],
                                                 ALU.subtract), diff_step, n + 1)
                fin(dve, nc.vector.tensor_scalar(d[:, 0:1], env.tile(raw + i)[:, 0:1], -1.0, None, ALU.mult), diff_step, n + 2)
                n += 2
                nc.vector.scalar_tensor_tensor(d, d, env.col("rw_mu", i), env.tile(raw + i), ALU.mult, ALU.add
                                               ).then_inc(lora_in_ready, 1)

        @block.scalar
        def _(act):
            act.wait_ge(lora_in_ready, 8)
            lo = env.tile(xwa)[0:HD]
            nc.scalar.activation(lo, lo, ACT.Tanh)
            nc.scalar.activation(env.tile(xg), env.tile(xg), ACT.Sigmoid)

    wa2 = env.words(W0, 0, 256)
    g2 = env.words(W0, 256, 256)
    with stage(env, "lora_in", "lora_done", "w_ready", "a_ready", "k_step") as (block, lora_in, lora_done, w_ready, a_ready, k_step):
        @block.sync
        def _(sp):
            sp.dma_start(wa2, dr["rw_wa2"]).then_inc(lora_in, 16)
            sp.dma_start(g2, dr["rw_g2"]).then_inc(lora_in, 16)

        @block.tensor
        def _(pe):
            pe.wait_ge(lora_in, 32)
            jobs = [(g2, xg, 0, P), (wa2, xwa, 0, HD), (wa2, xwa, HD, P)]
            for j, (w, x, lo, hi) in enumerate(jobs):
                for i in range(2):
                    c = ((2 * j + i) % 4) * T
                    if j == 2:
                        pe.wait_ge(w_ready, i + 1)
                    for n in range(2):
                        mm = nc.tensor.matmul(env.ps(c + n * BANK, c + (n + 1) * BANK), w[lo:hi, i * P:(i + 1) * P],
                                              env.tile(x, n * BANK, (n + 1) * BANK)[lo:hi], start=True, stop=True)
                    mm.then_inc(lora_done, 1)

        @block.scalar
        def _(act):
            for j in range(2):
                for i in range(2):
                    act.wait_ge(lora_done, 2 * j + i + 1)
                    c = (2 * j + i) * T
                    if j == 0:
                        nc.scalar.activation(env.tile(gate + i), env.ps(c, c + T), ACT.Copy).then_inc(w_ready, 1)
                    else:
                        nc.scalar.activation(env.tile(lw + i), env.ps(c, c + T), ACT.Sigmoid, bias=env.col("rw_w0", i)
                                             ).then_inc(w_ready, 1)
            for i in range(2):
                act.wait_ge(lora_done, 4 + i + 1)
                nc.scalar.activation(env.tile(a + i), env.ps(i * T, (i + 1) * T), ACT.Sigmoid, bias=env.col("rw_a0", i)
                                     ).then_inc(a_ready, 1)

        @block.vector
        def _(dve):
            for i in range(2):
                nc.vector.tensor_scalar(env.tile(kk + i), env.tile(k + i), env.col("rw_k_k", i), None, ALU.mult
                                        ).then_inc(k_step, 1)
            for i in range(2):
                dve.wait_ge(w_ready, 3 + i)
                nc.vector.tensor_scalar(env.tile(lw + i), env.tile(lw + i), -RWKV_RATE, None, ALU.mult)
            dve.wait_ge(k_step, 2)
            for i in range(2):
                dve.wait_ge(a_ready, i + 1)
                t = env.tile(W0 + 2)
                fin(dve, nc.vector.tensor_scalar(t, env.tile(a + i), env.col("rw_k_a", i), env.col("rw_k_a", i),
                                                 ALU.mult, ALU.subtract), k_step, 3 + 2 * i)
                fin(dve, nc.vector.scalar_tensor_tensor(env.tile(k + i), t, 1.0, env.tile(k + i), ALU.add, ALU.mult),
                    k_step, 4 + 2 * i)
    norm_stage(env, [((kk + i,), (kk + i,), None) for i in range(2)], env.const["ones64"], 1.0, "eps6", W0)

    bonus, cum, rev, mask = W0, W0 + 2, W0 + 4, W0 + 6
    small = Words(env, [(W0 + 7, T)])
    decay_cols, mid_next = small.take(16), small.take(16)
    chunked = lambda ap: ap.rearrange("p (c t) -> p c t", t=P)
    with stage(env, "mask_step", "cum_step", "rk_ready", "dots_done", "e_ready", "e_used", "mid_ready") as (
            block, mask_step, cum_step, rk_ready, dots_done, e_ready, e_used, mid_ready):
        @block.vector
        def _(dve):
            n = 0

            def step(ins):
                nonlocal n
                n += 1
                fin(dve, ins, cum_step, n)
            for i in range(2):
                step(nc.vector.tensor_tensor(env.tile(bonus + i), env.tile(r + i), env.tile(k + i), ALU.mult))
                nc.vector.tensor_scalar(env.tile(bonus + i), env.tile(bonus + i), env.col("rw_r_k", i), None, ALU.mult
                                        ).then_inc(rk_ready, 1)
                step(nc.vector.tensor_tensor(env.tile(a + i), env.tile(a + i), env.tile(kk + i), ALU.mult))
            write_restart_mask(env, dve, env.tile(mask), mask_step)
            for i in range(2):
                c3, r3 = chunked(env.tile(cum + i)), chunked(env.tile(rev + i))
                step(nc.vector.tensor_tensor_scan(env.tile(rev + i), env.tile(mask), env.tile(lw + i), 0.0, ALU.mult, ALU.add))
                mid = r3[:, :, HD - 1:HD]
                d, mn = decay_cols[:, i * NC:(i + 1) * NC], mid_next[:, i * NC:(i + 1) * NC]
                step(nc.vector.tensor_copy(mn, r3[:, :, HD - 1]))
                step(nc.vector.tensor_tensor(d, r3[:, :, P - 1], mn, ALU.subtract))
                ins = nc.vector.tensor_tensor(d[:, 0:NC - 1], d[:, 0:NC - 1], mn[:, 1:NC], ALU.add)
                ins.then_inc(mid_ready, 1)
                step(nc.vector.tensor_tensor(c3, r3, mid.broadcast_to([P, NC, P]), ALU.subtract))
                nc.vector.tensor_tensor(env.tile(lw + i), env.tile(cum + i), env.tile(lw + i), ALU.subtract
                                        ).then_inc(mid_ready, 1)
            for i in range(2):
                dve.wait_ge(dots_done, i + 1)
                nc.vector.tensor_tensor(env.tile(bonus + i), env.tile(v + i), env.ps(i * T, (i + 1) * T), ALU.mult)
            for i in range(2):
                dve.wait_ge(e_ready, 3 * i + 1)
                nc.vector.tensor_tensor(env.tile(kk + i), env.tile(kk + i), env.tile(lw + i), ALU.mult)
                dve.wait_ge(e_ready, 3 * i + 2)
                step(nc.vector.tensor_tensor(env.tile(k + i), env.tile(k + i), env.tile(rev + i), ALU.mult))
                step(nc.vector.tensor_tensor(env.tile(a + i), env.tile(a + i), env.tile(rev + i), ALU.mult))
                dve.wait_ge(e_ready, 3 * i + 3)
                nc.vector.tensor_tensor(env.tile(r + i), env.tile(r + i), env.tile(cum + i), ALU.mult)

        @block.tensor
        def _(pe):
            for i in range(2):
                pe.wait_ge(rk_ready, i + 1)
                for n in range(2):
                    c = i * T + n * BANK
                    mm = nc.tensor.matmul(env.ps(c, c + BANK), env.const["ones64"], env.tile(bonus + i, n * BANK, (n + 1) * BANK),
                                          start=True, stop=True)
                mm.then_inc(dots_done, 1)

        @block.scalar
        def _(act):
            for i in range(2):
                act.wait_ge(mid_ready, 2 * i + 2)
                nc.scalar.activation(env.tile(lw + i), env.tile(lw + i), ACT.Exp).then_inc(e_ready, 1)
                nc.scalar.activation(env.tile(rev + i), env.tile(cum + i), ACT.Exp, scale=-1.0).then_inc(e_ready, 1)
                act.wait_ge(e_ready, 3 * i + 2)
                nc.scalar.activation(env.tile(cum + i), env.tile(cum + i), ACT.Exp).then_inc(e_ready, 1)
            nc.scalar.activation(decay_cols, decay_cols, ACT.Exp)

    v_tok, k_tok, b_tok = R0, W0 + 2, W0 + 4
    token_major_stage(env, (v, v + 1), v_tok)
    token_major_stage(env, (k, k + 1), k_tok)
    token_major_stage(env, (a, a + 1), b_tok)
    room = Words(env, [(W0 + 6, T), (N0, 2 * T), (v, 2 * T), (xwa, 2 * T)])
    delta_chunks(env, room, "rwkv", {
        "aT": kk, "bT": a, "kT": k, "rT": r, "v_tok": v_tok, "k_tok": k_tok, "b_tok": b_tok, "out": out,
        "decay": lambda i, it: decay_cols[:, i * NC:(i + 1) * NC][:, bass.ds(it, 1)]})
    norm_stage(env, [((out + i,), (out + i,), [env.col("rw_lnx_g", i)]) for i in range(2)], env.const["ones64"], 1.0 / HD, "eps_lnx",
               W0 + 2, center=True, post=lambda gi, i: (ACT.Identity, env.col("rw_lnx_b", gi)))
    with stage(env, "sum_step") as (block, sum_step):
        @block.vector
        def _(dve):
            o = env.arena[:, out * T:(out + 2) * T]
            fin(dve, nc.vector.tensor_tensor(o, o, env.arena[:, bonus * T:(bonus + 2) * T], ALU.add), sum_step, 1)
            nc.vector.tensor_tensor(o, o, env.arena[:, gate * T:(gate + 2) * T], ALU.mult)



def conformer_in(env):
    nc, dr = env.nc, env.dram
    z = CF_H
    gemm_stage(env, [dr["w_in"][:, 2568:3080]], N0, KD, 2, copies_to(env, z, [ACT.Copy, ACT.Sigmoid]))
    with stage(env) as (block,):
        @block.vector
        def _(dve):
            nc.vector.tensor_tensor(env.arena[:, z * T:(z + 2) * T], env.arena[:, z * T:(z + 2) * T],
                                    env.arena[:, (z + 2) * T:(z + 4) * T], ALU.mult)


def conformer_conv(env, dve, tap_done):
    taps = 31
    for i in range(2):
        env.nc.vector.tensor_scalar(env.tile(CF_OUT + i), env.tile(CF_H + i), env.col("cf_conv_w", 2 * (taps - 1) + i),
                                    env.col("cf_conv_b", i), ALU.mult, ALU.add).then_inc(tap_done, 1)
    for back in range(1, taps):
        for i in range(2):
            dve.wait_ge(tap_done, 2 * back + i - 1)
            d = env.tile(CF_OUT + i, back)
            env.nc.vector.scalar_tensor_tensor(d, env.tile(CF_H + i, 0, T - back), env.col("cf_conv_w", 2 * (taps - 1 - back) + i),
                                               d, ALU.mult, ALU.add).then_inc(tap_done, 1)


def conformer_norm(env):
    norm_stage(env, [((CF_OUT, CF_OUT + 1), (CF_OUT, CF_OUT + 1), [env.col("cf_ln_g", i) for i in range(2)])],
               env.const["ones"], 1.0 / 256, "eps5", W0, center=True, post=lambda gi, i: (ACT.Silu, env.col("cf_ln_b", i)))



def add_to_residual(env, scale=None):
    def f(dve, g, half, wait, free, sems):
        wait(0)
        ins = None
        for m in range(2):
            c = half * 4 * BANK + m * T
            h = env.arena[:, H0 * T:(H0 + KD) * T][:, bass.ds(g * (2 * T) + m * T, T)]
            if scale is None:
                ins = env.nc.vector.tensor_tensor(h, h, env.ps(c, c + T), ALU.add)
            else:
                ins = env.nc.vector.scalar_tensor_tensor(h, h, scale, env.ps(c, c + T), ALU.mult, ALU.add)
        free(ins, 0)
    return {"vector": f}


def rms_of_h(env, gain, dst=N0):
    norm_stage(env, [(range(H0, H0 + KD), range(dst, dst + KD), [env.col(gain, k) for k in range(KD)])],
               env.const["ones"], 1.0 / D, "eps6", W0)


def rest_of_first_block(env):
    nc, dr = env.nc, env.dram
    gemm_stage(env, [dr["w_out"]], O0, KD, 4, add_to_residual(env))
    rms_of_h(env, "norm_ffn_g")

    hidden, kt = O0, 22
    raw = O0 + kt

    def gate_in(act, g, half, wait, free, sems):
        gate_raw, taps_done, act_done, used, gate_free, _ = sems
        for m in range(2):
            if m == 0:
                wait(0)
                act.wait_ge(used, g + 1)
            ins = nc.scalar.activation(env.tile(raw + m), env.ps(m * T, (m + 1) * T), ACT.Copy)
            if m == 0:
                ins.then_inc(gate_raw, 1)
            else:
                free(ins, 0)
        for m in range(2):
            act.wait_ge(taps_done, g * 2 + (m + 1))
            h = env.arena[:, hidden * T:(hidden + kt) * T][:, bass.ds(g * (2 * T) + m * T, T)]
            nc.scalar.activation(h, h, ACT.Silu).then_inc(act_done, 1)

    def conv_and_up(dve, g, half, wait, free, sems):
        gate_raw, taps_done, act_done, used, gate_free, _ = sems
        ncol = lambda tap, m: env.cols[:, env.cols_at["ffn_conv_w"] + tap * kt:env.cols_at["ffn_conv_w"] + (tap + 1) * kt][
            :, bass.ds(g * 2 + m, 1)]
        whole = env.arena[:, hidden * T:(hidden + kt) * T]
        for m in range(2):
            if m == 0:
                dve.wait_ge(gate_raw, g + 1)
            else:
                dve.wait_ge(gate_free, g + 2)
            x = env.tile(raw + m)
            at = lambda back: whole[:, bass.ds(g * (2 * T) + (m * T + back), T - back)]
            nc.vector.tensor_scalar(at(0), x, ncol(2, m), None, ALU.mult).then_inc(env.ffn_step, 1)
            dve.wait_ge(env.ffn_step, g * 4 + (2 * m + 1))
            nc.vector.scalar_tensor_tensor(at(1), x[:, 0:T - 1], ncol(1, m), at(1), ALU.mult, ALU.add).then_inc(env.ffn_step, 1)
            dve.wait_ge(env.ffn_step, g * 4 + (2 * m + 2))
            nc.vector.scalar_tensor_tensor(at(2), x[:, 0:T - 2], ncol(0, m), at(2), ALU.mult, ALU.add).then_inc(taps_done, 1)
        dve.wait_ge(taps_done, g * 2 + 2)
        dve.sem_inc(used, 1)
        dve.wait_ge(act_done, g * 2 + 2)
        wait(1)
        for m in range(2):
            h = whole[:, bass.ds(g * (2 * T) + m * T, T)]
            ins = nc.vector.tensor_tensor(h, h, env.ps(4 * BANK + m * T, 4 * BANK + (m + 1) * T), ALU.mult)
        free(ins, 1)
    gemm_stage(env, [dr["w_ffn_gate"], dr["w_ffn_up"]], N0, KD, 11, {"scalar": gate_in, "vector": conv_and_up},
               extra=("gate_raw", "taps_done", "act_done", "used"), start_with=("used",))
    gemm_stage(env, [dr["w_ffn_down"]], O0, kt, 4, add_to_residual(env))

    rms_of_h(env, "norm_ple_g")
    pt, gt = O0, O0 + 2
    with stage(env, "p_in") as (block, p_in):
        @block.sync
        def _(sp):
            sp.dma_start(env.arena[:, pt * T:(pt + 2) * T].rearrange("p (k t) -> p k t", k=2),
                         dr["pT"].rearrange("(k p) t -> p k t", p=P)).then_inc(p_in, 16)
            sp.wait_ge(p_in, 16)
    gemm_stage(env, [dr["w_ple_gate"]], N0, KD, 4, copies_to(env, gt, [ACT.Sigmoid] * 4))

    def times_gate(dve, g, half, wait, free, sems):
        wait(0)
        for m in range(2):
            c = half * 4 * BANK + m * T
            gate = env.tile(gt + 2 * g + m)
            ins = nc.vector.tensor_tensor(gate, gate, env.ps(c, c + T), ALU.mult)
        free(ins, 0)
        dve.wait_ge(sems[half], g // 2 + 2)
        for m in range(2):
            h = env.tile(H0 + 2 * g + m)
            nc.vector.tensor_tensor(h, h, env.tile(gt + 2 * g + m), ALU.add)
    gemm_stage(env, [dr["w_ple_proj"]], pt, 2, 4, {"vector": times_gate})
    rms_of_h(env, "final_norm_g", H0)



SSD_HEADS = 8
ALPHA = 2.0 ** 0.25


def ssd(env):
    nc, dr = env.nc, env.dram
    z, raw, xs, bm, cm = N0, R0, R0 + 8, R0 + 12, R0 + 14
    xs_tok, bm_tok, out = R0, R0 + 4, O0
    rows = lambda t: env.arena[0:SSD_HEADS, t * T:(t + 1) * T]
    dt_row, a_row = N0 + 4, N0 + 5
    gemm_stage(env, [dr["w_in_2"][:, 0:512]], H0, KD, 2, copies_to(env, z, [ACT.Silu] * 2))
    gemm_stage(env, [dr["w_in_2"][:, 512:1536]], H0, KD, 4, copies_to(env, raw, [ACT.Copy] * 4))
    conv_stage(env, [(raw + i, xs + i, [env.col("ssd_conv_w_2", 8 * j + i) for j in range(4)], env.col("ssd_conv_b_2", i))
                     for i in range(8)], 4, ACT.Silu)
    token_major_stage(env, range(xs, xs + 4), xs_tok)
    token_major_stage(env, (bm, bm + 1), bm_tok)
    small_rows_gemm(env, dr["w_in_2"][:, 1536:1544], H0, [(0, SSD_HEADS, 0)])
    softplus_stage(env, [(env.psum[0:SSD_HEADS, 0:T], rows(dt_row), rows(W0 + 2), 1.0, env.col("ssd_dt_bias_2")[0:SSD_HEADS])])

    small = Words(env, [(N0 + 6, 2 * T)])
    sel8 = small.take(SSD_HEADS * P)[0:SSD_HEADS]
    dt_tok, a_tok, rate = small.take(64), small.take(64), small.take(1)[0:SSD_HEADS]
    with stage(env, "sel_in", "mask_step", "rate_ready", "a_ready", "turned") as (block, sel_in, mask_step, rate_ready, a_ready, turned):
        @block.sync
        def _(sp):
            sp.dma_start(sel8, dr["sel8"]).then_inc(sel_in, 16)
            sp.wait_ge(sel_in, 16)

        @block.scalar
        def _(act):
            nc.scalar.activation(rate, env.col("ssd_a_log_2")[0:SSD_HEADS], ACT.Exp).then_inc(rate_ready, 1)

        @block.vector
        def _(dve):
            write_restart_mask(env, dve, rows(W0 + 2), mask_step)
            dve.wait_ge(rate_ready, 1)
            fin(dve, nc.vector.tensor_scalar(rows(W0 + 3), rows(dt_row), rate, -1.0, ALU.mult, ALU.mult), a_ready, 1)
            chunk_sums(env, dve, rows(a_row), rows(W0 + 3), rows(W0 + 2), a_ready, 2)
            dve.wait_ge(turned, 1)
            nc.vector.tensor_copy(dt_tok, env.ps(0, 64))
            nc.vector.tensor_copy(a_tok, env.ps(64, 128))

        @block.tensor
        def _(pe):
            pe.wait_ge(a_ready, 2)
            for r, c0 in ((dt_row, 0), (a_row, 64)):
                for c in range(NC):
                    mm = nc.tensor.matmul(env.ps(c0 + c * SSD_HEADS, c0 + (c + 1) * SSD_HEADS), rows(r)[:, c * P:(c + 1) * P],
                                          env.const["ident"][0:SSD_HEADS, 0:SSD_HEADS], start=True, stop=True)
            mm.then_inc(turned, 1)

    room = Words(env, [(W0, 8 * T)])
    bmc, cmc, btok, xdt, xds = room.take(256), room.take(256), room.take(256), room.take(512), room.take(512)
    mm_, ea, ce, cb, state, dcs, cd = (room.take(n) for n in (1024, 1024, 1024, 256, 512, 8, 8))
    two = lambda ap: ap.rearrange("p (i t) -> p i t", i=2)

    def fchunk(t0, n, it):
        return env.arena[:, t0 * T:(t0 + n) * T].rearrange("p (i t) -> p i t", i=n)[:, :, bass.ds(it * P, P)]

    def tchunk(t0, w, it):
        return env.arena[:, t0 * T:t0 * T + NC * w][:, bass.ds(it * w, w)]
    bank = lambda b, n=BANK: env.ps(b * BANK, b * BANK + n)
    with stage(env, "prep_ready", "xds_ready", "rows_done", "cb_done", "diff_ready", "exp_ready", "ea_ready", "m_ready",
               "ce_ready", "y_done", "s_done", "s_ready", "dve_step", "pool_step", "y_copied") as (
            block, prep_ready, xds_ready, rows_done, cb_done, diff_ready, exp_ready, ea_ready, m_ready, ce_ready, y_done,
            s_done, s_ready, dve_step, pool_step, y_copied):
        @block.gpsimd
        def _(pool):
            with pool.Fori(0, NC) as it:
                pool.wait_ge(s_done, it + 1)
                nc.gpsimd.tensor_copy(two(bmc), fchunk(bm, 2, it))
                nc.gpsimd.tensor_copy(two(cmc), fchunk(cm, 2, it))
                nc.gpsimd.tensor_copy(btok, tchunk(bm_tok, 256, it)).then_inc(prep_ready, 1)
                dt = dt_tok[:, bass.ds(it * SSD_HEADS, SSD_HEADS)].unsqueeze(2).broadcast_to([P, SSD_HEADS, HD])
                fin(pool, nc.gpsimd.tensor_tensor(by_head(xdt, HD), by_head(tchunk(xs_tok, 512, it), HD), dt, ALU.mult),
                    pool_step, it + 1)
                pool.wait_ge(exp_ready, it + 1)
                nc.gpsimd.tensor_tensor(by_head(xds, HD), by_head(xdt, HD), dcs.unsqueeze(2).broadcast_to([P, SSD_HEADS, HD]),
                                        ALU.mult).then_inc(xds_ready, 1)
                pool.wait_ge(ea_ready, it + 1)
                e4 = ea.rearrange("p (g h t) -> p g h t", g=2, h=4)
                c4 = two(cmc).unsqueeze(2).broadcast_to([P, 2, 4, P])
                nc.gpsimd.tensor_tensor(ce.rearrange("p (g h t) -> p g h t", g=2, h=4), e4, c4, ALU.mult).then_inc(ce_ready, 1)

        @block.tensor
        def _(pe):
            pe.sem_inc(s_done, 1)
            with pe.Fori(0, NC) as it:
                pe.wait_ge(s_ready, it + 1)
                for h in range(SSD_HEADS):
                    mm = nc.tensor.matmul(env.ps(h * P, (h + 1) * P), sel8[:, h * P:(h + 1) * P],
                                          rows(a_row)[:, bass.ds(it * P, P)], start=True, stop=True)
                mm.then_inc(rows_done, 1)
                pe.wait_ge(prep_ready, it + 1)
                for g in range(2):
                    mm = nc.tensor.matmul(bank(2)[:, g * P:(g + 1) * P], bmc[:, g * P:(g + 1) * P], cmc[:, g * P:(g + 1) * P],
                                          start=True, stop=True)
                mm.then_inc(cb_done, 1)
                pe.wait_ge(m_ready, it + 1)
                pe.wait_ge(ce_ready, it + 1)
                for h in range(SSD_HEADS):
                    lo = (h % 2) * HD
                    o = env.psum[lo:lo + HD, 3 * BANK + (h // 2) * P:3 * BANK + (h // 2 + 1) * P]
                    nc.tensor.matmul(o, xdt[:, h * HD:(h + 1) * HD], mm_[:, h * P:(h + 1) * P], start=True, stop=False)
                    mm = nc.tensor.matmul(o, state[:, h * HD:(h + 1) * HD], ce[:, h * P:(h + 1) * P], start=False, stop=True)
                mm.then_inc(y_done, 1)
                pe.wait_ge(xds_ready, it + 1)
                for g in range(2):
                    mm = nc.tensor.matmul(bank(4)[:, g * 256:(g + 1) * 256], btok[:, g * P:(g + 1) * P],
                                          xds[:, g * 256:(g + 1) * 256], start=True, stop=True)
                mm.then_inc(s_done, 1)

        @block.scalar
        def _(act):
            with act.Fori(0, NC) as it:
                act.wait_ge(diff_ready, it + 1)
                nc.scalar.activation(mm_, mm_, ACT.Exp)
                nc.scalar.activation(dcs, dcs, ACT.Exp).then_inc(exp_ready, 1)
                nc.scalar.activation(ea, env.ps(0, 2 * BANK), ACT.Exp).then_inc(ea_ready, 1)
                act.wait_ge(y_done, it + 1)
                nc.scalar.activation(fchunk(out, 4, it), bank(3).rearrange("p (i t) -> p i t", i=4), ACT.Copy
                                     ).then_inc(y_copied, 1)

        @block.vector
        def _(dve):
            fin(dve, nc.vector.memset(state, 0.0), s_ready, 1)
            with dve.Fori(0, NC) as it:
                dve.wait_ge(rows_done, it + 1)
                for h in range(SSD_HEADS):
                    nc.vector.tensor_scalar(mm_[:, h * P:(h + 1) * P], env.ps(h * P, (h + 1) * P),
                                            a_tok[:, bass.ds(it * SSD_HEADS + h, 1)], 0.0, ALU.subtract, ALU.min)
                nc.vector.tensor_tensor(dcs, env.ps(0, 2 * BANK).rearrange("p (h t) -> p h t", t=P)[:, :, P - 1],
                                        a_tok[:, bass.ds(it * SSD_HEADS, SSD_HEADS)], ALU.subtract).then_inc(diff_ready, 1)
                dve.wait_ge(cb_done, it + 1)
                fin(dve, nc.vector.tensor_tensor(two(cb), two(bank(2, 256)), rep(env.const["incl"], 2), ALU.mult), dve_step, it * 4 + 1)
                dve.wait_ge(exp_ready, it + 1)
                m4 = mm_.rearrange("p (g h t) -> p g h t", g=2, h=4)
                nc.vector.tensor_tensor(m4, m4, two(cb).unsqueeze(2).broadcast_to([P, 2, 4, P]), ALU.mult).then_inc(m_ready, 1)
                dve.wait_ge(ea_ready, it + 1)
                fin(dve, nc.vector.tensor_copy(cd, ea.rearrange("p (h t) -> p h t", t=P)[:, :, P - 1]), dve_step, it * 4 + 2)
                dve.wait_ge(y_done, it + 1)
                fin(dve, nc.vector.tensor_tensor(by_head(state, HD), by_head(state, HD),
                                                 cd.unsqueeze(2).broadcast_to([P, SSD_HEADS, HD]), ALU.mult),
                    dve_step, it * 4 + 3)
                dve.wait_ge(s_done, it + 2)
                fin(dve, nc.vector.tensor_tensor(state, state, bank(4), ALU.add), dve_step, it * 4 + 4)
                dve.wait_ge(y_copied, it + 1)
                dve.sem_inc(s_ready, 1)

    with stage(env, "skip_step") as (block, skip_step):
        @block.vector
        def _(dve):
            for i in range(4):
                o = env.tile(out + i)
                fin(dve, nc.vector.scalar_tensor_tensor(o, env.tile(xs + i), env.col("ssd_d_2", i), o, ALU.mult, ALU.add),
                    skip_step, i + 1)
                nc.vector.tensor_tensor(o, o, env.tile(z + i), ALU.mult)
    norm_stage(env, [(range(out, out + 4), range(out, out + 4), [env.col("ssd_norm_w_2", i) for i in range(4)])],
               env.const["ones"], 1.0 / 512, "eps5", W0)



def rglru(env):
    nc, dr = env.nc, env.dram
    raw, gelu, xc, rr, ii, la = R0, R0 + 2, R0 + 4, R0 + 6, R0 + 8, R0 + 10
    out = O0 + 6
    gemm_stage(env, [dr["w_in_2"][:, 1800:2312]], H0, KD, 2, copies_to(env, raw, [ACT.Copy, ACT.Gelu_apprx_tanh]))
    conv_stage(env, [(raw + i, xc + i, [env.col("rg_conv_w_2", 2 * j + i) for j in range(4)], env.col("rg_conv_b_2", i))
                     for i in range(2)], 4)
    w = env.words(W0, 0, 512)
    cols2 = [env.words(W0, 512 + 2 * i, 2) for i in range(6)]
    sp_col, z, s1, s2, acc, sp_part = cols2
    lam = env.cols[:, env.cols_at["rg_lambda_2"]:env.cols_at["rg_lambda_2"] + 2]
    with stage(env, "z_ready", "step") as (block, z_ready, step):
        @block.scalar
        def _(act):
            fin(act, nc.scalar.activation(s1, lam, ACT.Abs), z_ready, 1)
            nc.scalar.activation(z, s1, ACT.Exp, scale=-1.0).then_inc(z_ready, 1)

        @block.vector
        def _(dve):
            n = 0

            def do(ins):
                nonlocal n
                n += 1
                fin(dve, ins, step, n)
            dve.wait_ge(z_ready, 2)
            do(nc.vector.tensor_scalar(s1, z, 2.0, None, ALU.add))
            do(nc.vector.reciprocal(s1, s1))
            do(nc.vector.tensor_tensor(s1, s1, z, ALU.mult))
            do(nc.vector.tensor_tensor(s2, s1, s1, ALU.mult))
            do(nc.vector.memset(acc, 1.0 / 19))
            for k in range(17, 0, -2):
                do(nc.vector.tensor_tensor(acc, acc, s2, ALU.mult))
                do(nc.vector.tensor_scalar(acc, acc, 1.0 / k, None, ALU.add))
            do(nc.vector.tensor_tensor(acc, acc, s1, ALU.mult))
            do(nc.vector.tensor_scalar(sp_part, lam, -1.0, 0.0, ALU.mult, ALU.max))
            do(nc.vector.scalar_tensor_tensor(sp_col, acc, 2.0, sp_part, ALU.mult, ALU.add))
    with stage(env, "w_gates_in", "gates_done", "gates_ready", "la_ready", "f_ready", "step", "root_ready") as (
            block, w_gates_in, gates_done, gates_ready, la_ready, f_ready, step, root_ready):
        @block.sync
        def _(sp):
            sp.dma_start(w, dr["rg_w"]).then_inc(w_gates_in, 16)

        @block.tensor
        def _(pe):
            pe.wait_ge(w_gates_in, 16)
            for j in range(2):
                for i in range(2):
                    for n in range(2):
                        c = (2 * j + i) * T + n * BANK
                        mm = nc.tensor.matmul(env.ps(c, c + BANK), w[:, (2 * j + i) * P:(2 * j + i + 1) * P],
                                              env.tile(xc + i, n * BANK, (n + 1) * BANK), start=True, stop=True)
                    mm.then_inc(gates_done, 1)

        @block.scalar
        def _(act):
            for j, (dst, bias) in enumerate(((rr, "rg_ba_2"), (ii, "rg_bx_2"))):
                for i in range(2):
                    act.wait_ge(gates_done, 2 * j + i + 1)
                    c = (2 * j + i) * T
                    nc.scalar.activation(env.tile(dst + i), env.ps(c, c + T), ACT.Sigmoid, bias=env.col(bias, i)
                                         ).then_inc(gates_ready, 1)
            for i in range(2):
                act.wait_ge(la_ready, i + 1)
                nc.scalar.activation(env.tile(W0 + 2 + i), env.tile(la + i), ACT.Tanh).then_inc(f_ready, 1)
                nc.scalar.activation(env.tile(W0 + 4 + i), env.tile(la + i), ACT.Exp, scale=2.0).then_inc(f_ready, 1)
                nc.scalar.activation(env.tile(rr + i), env.tile(la + i), ACT.Exp).then_inc(f_ready, 1)
            for i in range(2):
                act.wait_ge(step, 2 + 3 * i + 2)
                nc.scalar.activation(env.tile(W0 + 2 + i), env.tile(W0 + 2 + i), ACT.Sqrt).then_inc(root_ready, 1)

        @block.vector
        def _(dve):
            for i in range(2):
                dve.wait_ge(gates_ready, i + 1)
                nc.vector.tensor_scalar(env.tile(la + i), env.tile(rr + i), sp_col[:, i:i + 1], -8.0, ALU.mult, ALU.mult
                                        ).then_inc(la_ready, 1)
            dve.sem_inc(step, 1)
            for i in range(2):
                dve.wait_ge(f_ready, 3 * i + 3)
                e, t = env.tile(W0 + 4 + i), env.tile(W0 + 2 + i)
                fin(dve, nc.vector.scalar_tensor_tensor(t, e, 1.0, t, ALU.add, ALU.mult), step, 2 + 3 * i)
                fin(dve, nc.vector.tensor_scalar(t, t, -1.0, None, ALU.mult), step, 3 + 3 * i)
                dve.wait_ge(gates_ready, 3 + i)
                nc.vector.tensor_tensor(env.tile(xc + i), env.tile(xc + i), env.tile(ii + i), ALU.mult).then_inc(step, 1)
            for i in range(2):
                dve.wait_ge(root_ready, i + 1)
                dve.wait_ge(step, 7 + 2 * i)
                x = env.tile(xc + i)
                fin(dve, nc.vector.tensor_tensor(x, x, env.tile(W0 + 2 + i), ALU.mult), step, 8 + 2 * i)
                fin(dve, nc.vector.tensor_tensor_scan(x, env.tile(rr + i), x, 0.0, ALU.mult, ALU.add), step, 9 + 2 * i)
                nc.vector.tensor_tensor(env.tile(out + i), x, env.tile(gelu + i), ALU.mult)



TWO_PI_HI = 6.28125
TWO_PI_LO = 2.0 * 3.141592653589793 - 6.28125
INT32 = mybir.dt.int32


def s5(env):
    nc, dr = env.nc, env.dram
    u, out = R0, O0 + 4
    ns = 8
    gemm_stage(env, [dr["w_in_2"][:, 1544:1800]], H0, KD, 1, copies_to(env, u, [ACT.Copy]))

    bre, bim, cre, cim, cr2, ci2 = R0 + 2, R0 + 3, R0 + 4, R0 + 5, R0 + 6, R0 + 7
    small = Words(env, [(N0, T)])
    names = ["step", "x", "y", "e", "em1", "rho", "sin", "cm1", "half", "t1", "t2", "t3", "ar", "ai", "inv", "cr", "ci",
             "cos", "zero8"]
    q = {n: small.take(ns) for n in names}
    turns = 10
    cn, sn = [small.take(ns) for _ in range(turns)], [small.take(ns) for _ in range(turns)]
    ki = small.take(ns).bitcast(INT32)
    lr = env.cols[:, env.cols_at["s5_lam_re_2"]:env.cols_at["s5_lam_re_2"] + ns]
    li = env.cols[:, env.cols_at["s5_lam_im_2"]:env.cols_at["s5_lam_im_2"] + ns]
    ls = env.cols[:, env.cols_at["s5_log_step_2"]:env.cols_at["s5_log_step_2"] + ns]
    v = nc.vector
    with stage(env, "mats_in", "act_done", "dve_step") as (block, mats_in, act_done, dve_step):
        @block.sync
        def _(sp):
            for name, t in (("s5_b_re", bre), ("s5_b_im", bim), ("s5_c_re", cre), ("s5_c_im", cim)):
                sp.dma_start(env.tile(t), dr[name]).then_inc(mats_in, 16)
            sp.wait_ge(mats_in, 64)

        @block.scalar
        def _(act):
            nc.scalar.activation(q["step"], ls, ACT.Exp).then_inc(act_done, 1)
            act.wait_ge(dve_step, 2)
            nc.scalar.activation(q["e"], q["x"], ACT.Exp).then_inc(act_done, 1)
            nc.scalar.activation(q["t1"], q["x"], ACT.Tanh, scale=0.5).then_inc(act_done, 1)
            act.wait_ge(dve_step, 9)
            nc.scalar.activation(q["sin"], q["y"], ACT.Sin).then_inc(act_done, 1)
            nc.scalar.activation(q["half"], q["y"], ACT.Sin, scale=0.5).then_inc(act_done, 1)

        @block.vector
        def _(dve):
            n = 0

            def do(ins):
                nonlocal n
                n += 1
                fin(dve, ins, dve_step, n)

            def mul(o, a, b):
                do(v.tensor_tensor(o, a, b, ALU.mult))
            dve.wait_ge(act_done, 1)
            mul(q["x"], lr, q["step"])
            mul(q["y"], li, q["step"])
            do(v.tensor_scalar(q["t2"], q["y"], 1.0 / (TWO_PI_HI + TWO_PI_LO), None, ALU.mult))
            do(v.tensor_copy(ki, q["t2"]))
            do(v.tensor_copy(q["t2"], ki))
            do(v.scalar_tensor_tensor(q["y"], q["t2"], -TWO_PI_HI, q["y"], ALU.mult, ALU.add))
            do(v.scalar_tensor_tensor(q["y"], q["t2"], -TWO_PI_LO, q["y"], ALU.mult, ALU.add))
            do(v.tensor_scalar(q["y"], q["y"], 3.1415925, -3.1415925, ALU.min, ALU.max))
            do(v.memset(q["zero8"], 0.0))
            assert n == 9
            dve.wait_ge(act_done, 5)
            do(v.scalar_tensor_tensor(q["em1"], q["e"], 1.0, q["t1"], ALU.add, ALU.mult))
            do(v.tensor_scalar(q["rho"], q["em1"], 1.0, None, ALU.add))
            mul(q["t2"], q["half"], q["half"])
            do(v.tensor_scalar(q["cm1"], q["t2"], -2.0, None, ALU.mult))
            do(v.tensor_scalar(q["cos"], q["cm1"], 1.0, None, ALU.add))
            mul(q["t1"], q["em1"], q["cos"])
            do(v.tensor_tensor(q["ar"], q["t1"], q["cm1"], ALU.add))
            mul(q["ai"], q["rho"], q["sin"])
            mul(q["t1"], lr, lr)
            mul(q["t2"], li, li)
            do(v.tensor_tensor(q["t1"], q["t1"], q["t2"], ALU.add))
            do(v.reciprocal(q["inv"], q["t1"]))
            mul(q["t1"], q["ar"], lr)
            mul(q["t2"], q["ai"], li)
            do(v.tensor_tensor(q["t1"], q["t1"], q["t2"], ALU.add))
            mul(q["cr"], q["t1"], q["inv"])
            mul(q["t1"], q["ai"], lr)
            mul(q["t2"], q["ar"], li)
            do(v.tensor_tensor(q["t1"], q["t1"], q["t2"], ALU.subtract))
            mul(q["ci"], q["t1"], q["inv"])
            do(v.tensor_copy(cn[0], q["cos"]))
            do(v.tensor_copy(sn[0], q["sin"]))
            for lv in range(1, turns):
                mul(q["t1"], sn[lv - 1], cn[lv - 1])
                mul(q["t2"], sn[lv - 1], sn[lv - 1])
                do(v.tensor_scalar(sn[lv], q["t1"], 2.0, None, ALU.mult))
                do(v.tensor_scalar(cn[lv], q["t2"], -2.0, 1.0, ALU.mult, ALU.add))
            dve.wait_ge(mats_in, 64)
            t3 = lambda t: env.tile(t).rearrange("p (k c) -> p k c", k=ns)
            b = lambda name: q[name].unsqueeze(2).broadcast_to([P, ns, P])
            mul(t3(cr2), t3(cre), b("cr"))
            mul(t3(W0), t3(cim), b("ci"))
            do(v.tensor_tensor(env.tile(cr2), env.tile(cr2), env.tile(W0), ALU.subtract))
            mul(t3(ci2), t3(cre), b("ci"))
            mul(t3(W0), t3(cim), b("cr"))
            do(v.scalar_tensor_tensor(env.tile(ci2), env.tile(ci2), -1.0, env.tile(W0), ALU.mult, ALU.subtract))

    ct, st_, gr, gi, t1, t2 = R0 + 8, R0 + 9, R0 + 10, R0 + 11, R0 + 12, R0 + 13
    hr, hi = (W0, W0 + 2), (W0 + 1, W0 + 3)
    with stage(env, "bu_done", "bu_read", "h_ready", "h_used", "dve_step", "rot_ready", "y_done") as (
            block, bu_done, bu_read, h_ready, h_used, dve_step, rot_ready, y_done):
        @block.tensor
        def _(pe):
            for s in range(ns):
                if s >= 1:
                    pe.wait_ge(bu_read, s)
                for j, b in enumerate((bre, bim)):
                    for n in range(2):
                        c = j * T + n * BANK
                        mm = nc.tensor.matmul(env.ps(c, c + BANK), env.tile(b, s * P, (s + 1) * P),
                                              env.tile(u + s // 4, n * BANK, (n + 1) * BANK), start=True, stop=True)
                mm.then_inc(bu_done, 1)
                pe.wait_ge(h_ready, s + 1)
                for j, (c_, h_) in enumerate(((cr2, hr), (ci2, hi))):
                    for n in range(2):
                        c = (2 + s // 4) * T + n * BANK
                        mm = nc.tensor.matmul(env.ps(c, c + BANK), env.tile(c_, s * P, (s + 1) * P),
                                              env.tile(h_[s % 2], n * BANK, (n + 1) * BANK),
                                              start=(s % 4 == 0 and j == 0), stop=(s % 4 == 3 and j == 1))
                mm.then_inc(h_used, 1)

        @block.vector
        def _(dve):
            n = 0

            def do(ins):
                nonlocal n
                n += 1
                fin(dve, ins, dve_step, n)

            def tt(o, a, b, op):
                do(v.tensor_tensor(o, a, b, op))
            for s in range(ns):
                C, S = env.tile(ct), env.tile(st_)
                v.memset(C[:, 0:1], 1.0)
                do(v.memset(S[:, 0:1], 0.0))
                for lv in range(turns):
                    w = 1 << lv
                    cw, sw = cn[lv][:, s:s + 1], sn[lv][:, s:s + 1]
                    v.tensor_scalar(env.tile(t1)[:, 0:w], S[:, 0:w], sw, None, ALU.mult)
                    do(v.tensor_scalar(env.tile(t2)[:, 0:w], C[:, 0:w], sw, None, ALU.mult))
                    v.scalar_tensor_tensor(C[:, w:2 * w], C[:, 0:w], cw, env.tile(t1)[:, 0:w], ALU.mult, ALU.subtract)
                    do(v.scalar_tensor_tensor(S[:, w:2 * w], S[:, 0:w], cw, env.tile(t2)[:, 0:w], ALU.mult, ALU.add))
                dve.wait_ge(bu_done, s + 1)
                br, bi = env.ps(0, T), env.ps(T, 2 * T)
                A, B, G, I = env.tile(t1), env.tile(t2), env.tile(gr), env.tile(gi)
                v.tensor_tensor(G, br, C, ALU.mult)
                tt(A, bi, S, ALU.mult)
                v.tensor_tensor(I, bi, C, ALU.mult)
                ins = v.tensor_tensor(B, br, S, ALU.mult)
                fin(dve, ins, bu_read, s + 1)
                v.tensor_tensor(G, G, A, ALU.add)
                tt(I, I, B, ALU.subtract)
                rho = q["rho"][:, s:s + 1].broadcast_to([P, T])
                v.tensor_tensor_scan(G, rho, G, 0.0, ALU.mult, ALU.add)
                do(v.tensor_tensor_scan(I, rho, I, 0.0, ALU.mult, ALU.add))
                if s >= 2:
                    dve.wait_ge(h_used, s - 1)
                R, J = env.tile(hr[s % 2]), env.tile(hi[s % 2])
                v.tensor_tensor(R, G, C, ALU.mult)
                v.tensor_tensor(A, I, S, ALU.mult)
                v.tensor_tensor(J, G, S, ALU.mult)
                tt(B, I, C, ALU.mult)
                v.tensor_tensor(R, R, A, ALU.subtract)
                v.tensor_tensor(J, J, B, ALU.add).then_inc(h_ready, 1)
            for i in range(2):
                dve.wait_ge(h_used, 4 * i + 4)
                c = (2 + i) * T
                v.scalar_tensor_tensor(env.tile(out + i), env.tile(u + i), env.col("s5_d_2", i), env.ps(c, c + T),
                                       ALU.mult, ALU.add).then_inc(y_done, 1)

        @block.scalar
        def _(act):
            for i in range(2):
                act.wait_ge(y_done, i + 1)
                nc.scalar.activation(env.tile(out + i), env.tile(out + i), ACT.Gelu_apprx_tanh)

    sig = R0 + 8

    def glu(act, g, half, wait, free, sems):
        wait(0)
        for m in range(2):
            c = half * 4 * BANK + m * T
            ins = nc.scalar.activation(env.tile(sig + m), env.ps(c, c + T), ACT.Sigmoid, bias=env.col("s5_glu_b_2", m))
        free(ins, 0)
    gemm_stage(env, [dr["s5_glu_w_2"]], out, 2, 1, {"scalar": glu})
    with stage(env) as (block,):
        @block.vector
        def _(dve):
            o = env.arena[:, out * T:(out + 2) * T]
            v.tensor_tensor(o, o, env.arena[:, sig * T:(sig + 2) * T], ALU.mult)



def ln_of_h(env, name):
    norm_stage(env, [(range(H0, H0 + KD), range(H0, H0 + KD), [env.col(f"{name}_g_2", k) for k in range(KD)])],
               env.const["ones"], 1.0 / D, "eps5", W0, center=True, post=lambda gi, i: (ACT.Identity, env.col(f"{name}_b_2", i)))


MEM = 256
XA_SCALE = 1.0 / 16.0


def attention(env):
    nc, dr = env.nc, env.dram
    mem, kf, vt, qf, pt, of = R0 + 8, R0 + 10, R0 + 12, N0, R0, O0
    mem3 = env.arena[:, mem * T:(mem + 2) * T].rearrange("p (k t) -> p k t", k=KD)
    kf3 = env.arena[:, kf * T:(kf + 2) * T].rearrange("p (k t) -> p k t", k=KD)
    vt3 = env.arena[:, vt * T:(vt + 2) * T].rearrange("p (m f) -> p m f", m=2)
    with stage(env, "mem_in") as (block, mem_in):
        @block.sync
        def _(sp):
            sp.dma_start(mem3, dr["memT"].rearrange("(k p) t -> p k t", p=P)).then_inc(mem_in, 16)
            sp.wait_ge(mem_in, 16)

    gemm_stage(env, [dr["xa_wq_2"]], H0, KD, 4, copies_to(env, qf, [ACT.Copy] * 4))

    def keys(w, s):
        for m in range(2):
            for k in range(KD):
                mm = nc.tensor.matmul(env.ps(s * 4 * BANK + m * MEM, s * 4 * BANK + (m + 1) * MEM),
                                      w[:, k, m * P:(m + 1) * P], mem3[:, k, :], start=(k == 0), stop=(k == KD - 1))
        return mm

    def take_keys(act, g, half, wait, free, sems):
        wait(0)
        free(nc.scalar.activation(kf3[:, 2 * g:2 * g + 2, :], env.ps(half * 4 * BANK, half * 4 * BANK + 2 * MEM)
                                  .rearrange("p (m t) -> p m t", m=2), ACT.Copy), 0)
    gemm_stage(env, [dr["xa_wk_2"]], None, KD, 4, {"scalar": take_keys}, product=keys)

    def values(w, s):
        for m in range(2):
            for k in range(KD):
                mm = nc.tensor.matmul(env.ps(s * 4 * BANK + m * UNIT_M, s * 4 * BANK + (m + 1) * UNIT_M),
                                      mem3[:, k, m * P:(m + 1) * P], w[:, k, :], start=(k == 0), stop=(k == KD - 1))
        return mm

    def take_values(act, g, half, wait, free, sems):
        wait(0)
        free(nc.scalar.activation(vt3[:, :, g * UNIT_M:(g + 1) * UNIT_M], env.ps(half * 4 * BANK, half * 4 * BANK + 2 * UNIT_M)
                                  .rearrange("p (m f) -> p m f", m=2), ACT.Copy), 0)
    gemm_stage(env, [dr["xa_wv_2"]], None, KD, 4, {"scalar": take_values}, product=values)

    room = Words(env, [(W0, 8 * T)])
    qs, sc, mx, sums, inv = room.take(KD * P), room.take(HEADS * MEM), room.take(4), room.take(4), room.take(4)
    qs3 = qs.rearrange("p (k t) -> p k t", k=KD)
    sc3 = sc.rearrange("p (h m) -> p h m", h=HEADS)
    q3 = env.arena[:, qf * T:(qf + KD) * T].rearrange("p (k t) -> p k t", k=KD)
    p3 = env.arena[:, pt * T:(pt + 8) * T].rearrange("p (j t) -> p j t", j=8)
    with stage(env, "q_ready", "scores_done", "max_step", "exp_ready", "norm_step", "turned", "taken", "scores_free") as (
            block, q_ready, scores_done, max_step, exp_ready, norm_step, turned, taken, scores_free):
        @block.gpsimd
        def _(pool):
            with pool.Fori(0, NC) as it:
                pool.wait_ge(scores_free, it + 1)
                nc.gpsimd.tensor_copy(qs3, q3[:, :, bass.ds(it * P, P)]).then_inc(q_ready, 1)

        @block.tensor
        def _(pe):
            pe.sem_inc(scores_free, 1)
            pe.sem_inc(taken, 1)
            with pe.Fori(0, NC) as it:
                pe.wait_ge(q_ready, it + 1)
                for h in range(HEADS):
                    for k in range(2):
                        mm = nc.tensor.matmul(env.ps(h * MEM, (h + 1) * MEM), qs3[:, 2 * h + k, :], kf3[:, 2 * h + k, :],
                                              start=(k == 0), stop=(k == 1))
                mm.then_inc(scores_done, 1)
                pe.wait_ge(taken, it + 1)
                pe.wait_ge(norm_step, it * 2 + 2)
                for j in range(2):
                    for h in range(HEADS):
                        c = 2 * BANK + (j * HEADS + h) * P
                        mm = nc.tensor.transpose(env.ps(c, c + P), sc3[:, h, j * P:(j + 1) * P], env.const["ident"])
                mm.then_inc(turned, 1)

        @block.vector
        def _(dve):
            with dve.Fori(0, NC) as it:
                dve.wait_ge(scores_done, it + 1)
                fin(dve, nc.vector.tensor_reduce(mx, env.ps(0, 2 * BANK).rearrange("p (h m) -> p h m", h=HEADS), AX_X, ALU.max),
                    max_step, it * 2 + 1)
                nc.vector.tensor_scalar(mx, mx, -XA_SCALE, None, ALU.mult).then_inc(max_step, 1)
                dve.wait_ge(exp_ready, it + 1)
                fin(dve, nc.vector.reciprocal(inv, sums), norm_step, it * 2 + 1)
                nc.vector.tensor_tensor(sc3, sc3, inv.unsqueeze(2).broadcast_to([P, HEADS, MEM]), ALU.mult).then_inc(norm_step, 1)

        @block.scalar
        def _(act):
            with act.Fori(0, NC) as it:
                act.wait_ge(max_step, it * 2 + 2)
                for h in range(HEADS):
                    ins = nc.scalar.activation(sc3[:, h, :], env.ps(h * MEM, (h + 1) * MEM), ACT.Exp, scale=XA_SCALE,
                                               bias=mx[:, h:h + 1], accum_out=sums[:, h:h + 1])
                ins.then_inc(exp_ready, 1)
                act.wait_ge(turned, it + 1)
                act.wait_ge(exp_ready, it + 1)
                nc.scalar.activation(p3[:, :, bass.ds(it * P, P)], env.ps(2 * BANK, 4 * BANK)
                                     .rearrange("p (j t) -> p j t", j=8), ACT.Copy).then_inc(taken, 1)
                act.sem_inc(scores_free, 1)

    with stage(env, "pv_done", "pv_free") as (block, pv_done, pv_free):
        @block.tensor
        def _(pe):
            for i in range(KD):
                h = i // 2
                if i >= 4:
                    pe.wait_ge(pv_free, i - 3)
                for n in range(2):
                    c = (i % 4) * T + n * BANK
                    for j in range(2):
                        mm = nc.tensor.matmul(env.ps(c, c + BANK), vt3[:, j, i * P:(i + 1) * P],
                                              p3[:, j * HEADS + h, n * BANK:(n + 1) * BANK], start=(j == 0), stop=(j == 1))
                mm.then_inc(pv_done, 1)

        @block.scalar
        def _(act):
            for i in range(KD):
                act.wait_ge(pv_done, i + 1)
                c = (i % 4) * T
                nc.scalar.activation(env.tile(of + i), env.ps(c, c + T), ACT.Copy).then_inc(pv_free, 1)

    gemm_stage(env, [dr["xa_wo_2"]], of, KD, 4, add_to_residual(env, ALPHA))
    ln_of_h(env, "ln2")


def mlp(env):
    nc, dr = env.nc, env.dram
    hidden, kt = N0, 32

    def at(g, m):
        return env.arena[:, hidden * T:(hidden + kt) * T][:, bass.ds(g * (2 * T) + m * T, T)]

    def relu(act, g, half, wait, free, sems):
        turn = wait(0)
        for m in range(2):
            c = half * 4 * BANK + m * T
            ins = nc.scalar.activation(at(g, m), env.ps(c, c + T), ACT.Relu)
        free(ins, 0)
        act.wait_ge(sems[1 + half], turn + 2)
        act.sem_inc(sems[0], 1)

    def square(dve, g, half, wait, free, sems):
        dve.wait_ge(sems[0], g + 1)
        for m in range(2):
            nc.vector.tensor_tensor(at(g, m), at(g, m), at(g, m), ALU.mult)
    gemm_stage(env, [dr["mlp_w1_2"]], H0, KD, 16, {"scalar": relu, "vector": square}, extra=("relu_ready",))
    gemm_stage(env, [dr["mlp_w2_2"]], hidden, kt, 4, add_to_residual(env, ALPHA))
    ln_of_h(env, "ln3")


def second_block(env):
    ssd(env)
    s5(env)
    rglru(env)
    gemm_stage(env, [env.dram["w_out_2"]], O0, KD, 4, add_to_residual(env, ALPHA))
    ln_of_h(env, "ln1")
    attention(env)
    mlp(env)


def extra_arrays(x, arrays):
    import numpy as np
    rg = np.zeros((P, 4, P), np.float32)
    for j, name in enumerate(("rg_wa_2", "rg_wx_2")):
        for b in range(4):
            lo = (b % 2) * HD
            rg[lo:lo + HD, 2 * j + b // 2, lo:lo + HD] = x[name][0, b]
    arrays["rg_w"] = rg.reshape(P, -1)
    for part in ("re", "im"):
        b = np.zeros((P, 8, P), np.float32)
        c = np.zeros((P, 8, P), np.float32)
        for g in range(16):
            s, e = g // 2, g % 2
            ch = 32 * (s % 4) + 16 * e
            b[ch:ch + 16, s, e * HD:(e + 1) * HD] = x[f"s5_b_{part}_2"][0, g].T
            c[e * HD:(e + 1) * HD, s, ch:ch + 16] = x[f"s5_c_{part}_2"][0, g].T
        arrays[f"s5_b_{part}"] = b.reshape(P, -1)
        arrays[f"s5_c_{part}"] = c.reshape(P, -1)
    arrays["sel8"] = np.repeat(np.eye(8, dtype=np.float32), P, axis=1)


CONSTS = ["ident", "ones", "ones64", "incl", "strict"] + [f"level{i}" for i in range(LEVELS)]


def build(nc, dram, cols_at, n_cols, out):
    with ExitStack() as ctx:
        env = Env()
        env.nc, env.dram, env.cols_at, env.stages, env.units = nc, dram, cols_at, 0, 0
        env.arena = ctx.enter_context(nc.sbuf_tensor("arena", [P, TILES * T], F32))
        env.cols = ctx.enter_context(nc.sbuf_tensor("cols_sb", [P, n_cols], F32))
        env.psum = ctx.enter_context(nc.psum_tensor("psum", [P, 8 * BANK], F32))
        env.const = {}
        for name in CONSTS:
            env.const[name] = ctx.enter_context(nc.sbuf_tensor(f"{name}_sb", [P, P], F32))[:, :]
        sel_sb = ctx.enter_context(nc.sbuf_tensor("sel_sb", [HEADS, 6 * P], F32))
        env.sel = sel_sb[:, :]
        env.wslot = lambda s: env.arena[:, (W0 + 2 * s) * T:(W0 + 2 * s + 2) * T]
        env.w_in = [ctx.enter_context(nc.semaphore(f"w_in{s}")) for s in range(SLOTS)]
        env.unit_done = ctx.enter_context(nc.semaphore("unit_done"))
        env.ffn_step = ctx.enter_context(nc.semaphore("ffn_step"))
        with stage(env, "consts_in") as (block, consts_in):
            @block.sync
            def _(sp):
                n = 0
                for name in CONSTS:
                    sp.dma_start(env.const[name], dram[name]).then_inc(consts_in, 16)
                    n += 16
                sp.dma_start(env.sel, dram["sel"]).then_inc(consts_in, 16)
                n += 16
                sp.dma_start(env.cols[:, :], dram["cols"]).then_inc(consts_in, 16)
                sp.dma_start(env.arena[:, H0 * T:(H0 + KD) * T].rearrange("p (k t) -> p k t", k=KD),
                             dram["xT"].rearrange("(k p) t -> p k t", p=P)).then_inc(consts_in, 16)
                sp.wait_ge(consts_in, n + 32)
        steps = [first_norm_and_gmlp, conformer_in, delta_net, rwkv, rest_of_first_block, second_block]
        for s in steps:
            s(env)
        with stage(env, "out_done") as (block, out_done):
            @block.sync
            def _(sp):
                sp.dma_start(out.rearrange("(k p) t -> p k t", p=P),
                             env.arena[:, H0 * T:(H0 + KD) * T].rearrange("p (k t) -> p k t", k=KD)).then_inc(out_done, 16)
                sp.wait_ge(out_done, 16)



def constants():
    import numpy as np
    i = np.arange(P)
    s, t = i[:, None], i[None, :]
    blocks = {
        "ident": s == t,
        "ones": np.ones((P, P)),
        "ones64": s // HD == t // HD,
        "incl": s <= t,
        "strict": s < t,
    }
    for lv in range(LEVELS):
        blocks[f"level{lv}"] = (s >> (lv + 1) == t >> (lv + 1)) & ((t >> lv) % 2 == 1) & ((s >> lv) % 2 == 0)
    h = np.arange(HEADS)[:, None]
    blocks["sel"] = np.concatenate([(h == j) & (i[None] >= 0) for j in range(HEADS)]
                                   + [h == 2 * j + i[None] // HD for j in range(2)], axis=1)
    return {k: np.ascontiguousarray(v.astype(np.float32)) for k, v in blocks.items()}


def tiles_of(v):
    import numpy as np
    v = np.asarray(v).reshape(-1)
    n = -(-v.size // P)
    out = np.zeros(n * P, v.dtype)
    out[:v.size] = v
    return out.reshape(n, P).T


def column_layout(inputs):
    import numpy as np
    one = np.ones(P, np.float32)
    cols = {}
    for name in ["norm_mix_g", "gmlp_v_g", "gmlp_v_b", "norm_ffn_g", "norm_ple_g", "final_norm_g", "rw_mu", "rw_w0",
                 "rw_a0", "rw_k_k", "rw_k_a", "rw_r_k", "rw_lnx_g", "rw_lnx_b", "cf_conv_b", "cf_ln_g", "cf_ln_b",
                 "ssd_conv_b_2", "ssd_norm_w_2", "s5_d_2", "s5_glu_b_2", "s5_lam_re_2", "s5_lam_im_2", "rg_conv_b_2",
                 "rg_ba_2", "rg_bx_2", "rg_lambda_2", "ln1_g_2", "ln1_b_2", "ln2_g_2", "ln2_b_2", "ln3_g_2", "ln3_b_2",
                 "dn_a_log", "dn_dt_bias", "ssd_dt_bias_2", "ssd_a_log_2"]:
        cols[name] = tiles_of(inputs[name])
    cols["dn_o_g"] = tiles_of(np.tile(np.asarray(inputs["dn_o_g"])[0], 2))
    cols["ssd_d_2"] = tiles_of(np.repeat(np.asarray(inputs["ssd_d_2"])[0], HD))
    cols["s5_log_step_2"] = tiles_of(np.repeat(np.asarray(inputs["s5_log_step_2"])[0], HD))
    for name in ["dn_conv_w", "cf_conv_w", "ffn_conv_w", "ssd_conv_w_2", "rg_conv_w_2"]:
        w = np.asarray(inputs[name])[0]
        cols[name] = np.concatenate([tiles_of(r) for r in w], axis=1)
    for name, value in [("eps6", 1e-6), ("eps5", 1e-5), ("eps_lnx", 64e-5), ("one", 1.0), ("zero", 0.0), ("minus_one", -1.0)]:
        cols[name] = tiles_of(one * np.float32(value))
    cols["half0"] = tiles_of((np.arange(P) < HD).astype(np.float32))
    cols["half1"] = tiles_of((np.arange(P) >= HD).astype(np.float32))
    return cols


def kernel(**inputs):
    import numpy as np
    import concourse.bacc as bacc
    from concourse.bass_utils import run_bass_kernel_spmd

    nc = bacc.Bacc("TRN2", target_bir_lowering=False, num_devices=1)
    x = {k: np.asarray(v) for k, v in inputs.items()}
    cols = column_layout(x)
    at, n = {}, 0
    for k, v in cols.items():
        at[k] = n
        n += v.shape[1]
    arrays = {"cols": np.concatenate(list(cols.values()), axis=1), "xT": x["x"][0].T, "memT": x["mem_2"][0].T,
              "pT": x["p"][0, 0].T}
    arrays.update(constants())
    arrays["gmlp_w_sT"] = x["gmlp_w_s"][0].transpose(2, 0, 1).reshape(P, -1)
    arrays["gmlp_b_s"] = x["gmlp_b_s"][0].reshape(1, -1)
    for name in ["w_in", "w_out", "w_ffn_gate", "w_ffn_up", "w_ffn_down", "w_ple_gate", "w_ple_proj", "w_in_2", "w_out_2",
                 "xa_wq_2", "xa_wk_2", "xa_wv_2", "xa_wo_2", "mlp_w1_2", "mlp_w2_2", "s5_glu_w_2", "rw_g2"]:
        arrays[name] = x[name][0]
    arrays["rw_wa2"] = np.concatenate([x["rw_w2"][0], x["rw_a2"][0]], axis=0)
    extra_arrays(x, arrays)
    arrays = {k: np.ascontiguousarray(v) for k, v in arrays.items()}
    dram = {k: nc.dram_tensor(k, v.shape, F32, kind="ExternalInput").ap() for k, v in arrays.items()}
    out = nc.dram_tensor("outT", (D, T), F32, kind="ExternalOutput").ap()
    build(nc, dram, at, n, out)
    r = run_bass_kernel_spmd(nc, [arrays], core_ids=[0])
    return np.ascontiguousarray(r.results[0]["outT"].T)[None]
```
